# Optimizing a Trainium2 kernel written in Bass

```python
import math
import jax
import jax.numpy as jnp
from jax import lax
import numpy as np

D_MODEL = 1024
BATCH = 1
SEQ = 512
DEPTH = 2

HEAD_DIM = 64
SB_HEADS = 8
SWA_HEADS = 8
SWA_KV_HEADS = 2
SWA_GROUP = SWA_HEADS // SWA_KV_HEADS
WINDOW = 128
BLOCK = 128
D_FF = 4 * D_MODEL
ROPE_THETA = 10000.0
EPS = 1e-6
NEG = -1e30

SB_W = SB_HEADS * HEAD_DIM
SWA_Q_W = SWA_HEADS * HEAD_DIM
SWA_KV_W = SWA_KV_HEADS * HEAD_DIM
MIX_W = SB_W + SWA_Q_W
IN_W = 3 * SB_W + SWA_Q_W + 2 * SWA_KV_W

kernel_name = "hybrid_stickbreak_swa_sink_block"

def rmsnorm(x, g):
    xf = x.astype(jnp.float32)
    y = xf * lax.rsqrt(jnp.mean(xf * xf, axis=-1, keepdims=True) + EPS)
    return (y * g.astype(jnp.float32)).astype(x.dtype)

def rope(x, positions):
    half = HEAD_DIM // 2
    inv_freq = 1.0 / (ROPE_THETA ** (jnp.arange(half, dtype=jnp.float32) * (2.0 / HEAD_DIM)))
    ang = positions.astype(jnp.float32)[:, None] * inv_freq[None, :]
    cos = jnp.cos(ang)[None, :, None, :]
    sin = jnp.sin(ang)[None, :, None, :]
    xf = x.astype(jnp.float32)
    x1, x2 = xf[..., :half], xf[..., half:]
    out = jnp.concatenate([x1 * cos - x2 * sin, x2 * cos + x1 * sin], axis=-1)
    return out.astype(x.dtype)

def stick_breaking_attention(q, k, v):
    B, S, H, D = q.shape
    scale = 1.0 / math.sqrt(D)
    qh = jnp.transpose(q, (0, 2, 1, 3))
    kh = jnp.transpose(k, (0, 2, 1, 3))
    vh = jnp.transpose(v, (0, 2, 1, 3)).astype(jnp.float32)
    outs = []
    for i in range(S // BLOCK):
        end = (i + 1) * BLOCK
        qb = qh[:, :, i * BLOCK:end]
        z = jnp.einsum('bhqd,bhkd->bhqk', qb, kh[:, :, :end]).astype(jnp.float32) * scale
        t_pos = i * BLOCK + jnp.arange(BLOCK)[:, None]
        s_pos = jnp.arange(end)[None, :]
        strict = s_pos < t_pos
        log_beta = jax.nn.log_sigmoid(z)
        log_1m = jnp.where(strict, -jax.nn.softplus(z), 0.0)
        suffix = lax.cumsum(log_1m, axis=3, reverse=True) - log_1m
        a = jnp.where(strict, jnp.exp(log_beta + suffix), 0.0)
        outs.append(jnp.einsum('bhqk,bhkd->bhqd', a, vh[:, :, :end]))
    o = jnp.concatenate(outs, axis=2)
    return jnp.transpose(o, (0, 2, 1, 3)).astype(v.dtype)

def sliding_window_sink_attention(q, k, v, sinks):
    B, S, Hq, D = q.shape
    nblk = S // BLOCK
    scale = 1.0 / math.sqrt(D)
    qb = q.reshape(B, nblk, BLOCK, SWA_KV_HEADS, SWA_GROUP, D)
    pad = ((0, 0), (BLOCK, 0), (0, 0), (0, 0))
    kp = jnp.pad(k, pad).reshape(B, nblk + 1, BLOCK, SWA_KV_HEADS, D)
    vp = jnp.pad(v, pad).reshape(B, nblk + 1, BLOCK, SWA_KV_HEADS, D)
    kb = jnp.concatenate([kp[:, :-1], kp[:, 1:]], axis=2)
    vb = jnp.concatenate([vp[:, :-1], vp[:, 1:]], axis=2)
    s = jnp.einsum('bnqkgd,bnskd->bnkgqs', qb, kb).astype(jnp.float32) * scale
    q_rel = BLOCK + jnp.arange(BLOCK)[:, None]
    k_rel = jnp.arange(2 * BLOCK)[None, :]
    diff = q_rel - k_rel
    k_abs = (jnp.arange(nblk)[:, None, None] - 1) * BLOCK + k_rel[None]
    mask = (diff >= 0)[None] & (diff < WINDOW)[None] & (k_abs >= 0)
    mask = mask[None, :, None, None]
    s = jnp.where(mask, s, NEG)
    sink = sinks.astype(jnp.float32).reshape(1, 1, SWA_KV_HEADS, SWA_GROUP, 1, 1)
    m = jnp.maximum(jnp.max(s, axis=-1, keepdims=True), sink)
    p = jnp.where(mask, jnp.exp(s - m), 0.0)
    probs = p / (jnp.sum(p, axis=-1, keepdims=True) + jnp.exp(sink - m))
    o = jnp.einsum('bnkgqs,bnskd->bnqkgd', probs, vb.astype(jnp.float32))
    return o.reshape(B, S, Hq, D).astype(v.dtype)

def setup_inputs(seed: int = 0) -> dict:
    key = jax.random.key(seed)
    ks = jax.random.split(key, 12)
    f32 = jnp.float32
    x = jax.random.normal(ks[0], (BATCH, SEQ, D_MODEL), f32)
    positions = jnp.arange(SEQ, dtype=jnp.int32)
    attn_norm = 1.0 + 0.02 * jax.random.normal(ks[1], (DEPTH, D_MODEL), f32)
    w_in = jax.random.normal(ks[2], (DEPTH, D_MODEL, IN_W), f32) * D_MODEL ** -0.5
    sb_norm = 1.0 + 0.02 * jax.random.normal(ks[3], (DEPTH, SB_W), f32)
    swa_norm = 1.0 + 0.02 * jax.random.normal(ks[4], (DEPTH, SWA_Q_W), f32)
    sinks = 0.5 * jax.random.normal(ks[5], (DEPTH, SWA_HEADS), f32)
    w_out = jax.random.normal(ks[6], (DEPTH, MIX_W, D_MODEL), f32) * MIX_W ** -0.5
    mlp_norm = 1.0 + 0.02 * jax.random.normal(ks[7], (DEPTH, D_MODEL), f32)
    w_up = jax.random.normal(ks[8], (DEPTH, D_MODEL, D_FF), f32) * D_MODEL ** -0.5
    w_down = jax.random.normal(ks[9], (DEPTH, D_FF, D_MODEL), f32) * D_FF ** -0.5
    final_norm = 1.0 + 0.02 * jax.random.normal(ks[10], (D_MODEL,), f32)
    return {"x": x, "positions": positions, "attn_norm": attn_norm, "w_in": w_in,
            "sb_norm": sb_norm, "swa_norm": swa_norm, "sinks": sinks, "w_out": w_out,
            "mlp_norm": mlp_norm, "w_up": w_up, "w_down": w_down, "final_norm": final_norm}

def reference(x, positions, attn_norm, w_in, sb_norm, swa_norm, sinks, w_out,
              mlp_norm, w_up, w_down, final_norm):
    B, S, _ = x.shape
    splits = np.cumsum([SB_W, SB_W, SB_W, SWA_Q_W, SWA_KV_W]).tolist()
    for l in range(DEPTH):
        h = rmsnorm(x, attn_norm[l])
        proj = jnp.einsum('bsd,de->bse', h, w_in[l])
        sb_q, sb_k, sb_v, sw_q, sw_k, sw_v = jnp.split(proj, splits, axis=-1)
        sb_o = stick_breaking_attention(sb_q.reshape(B, S, SB_HEADS, HEAD_DIM),
                                        sb_k.reshape(B, S, SB_HEADS, HEAD_DIM),
                                        sb_v.reshape(B, S, SB_HEADS, HEAD_DIM))
        sw_q = rope(sw_q.reshape(B, S, SWA_HEADS, HEAD_DIM), positions)
        sw_k = rope(sw_k.reshape(B, S, SWA_KV_HEADS, HEAD_DIM), positions)
        sw_o = sliding_window_sink_attention(sw_q, sw_k,
                                             sw_v.reshape(B, S, SWA_KV_HEADS, HEAD_DIM),
                                             sinks[l])
        mix = jnp.concatenate([rmsnorm(sb_o.reshape(B, S, SB_W), sb_norm[l]),
                               rmsnorm(sw_o.reshape(B, S, SWA_Q_W), swa_norm[l])], axis=-1)
        x = x + jnp.einsum('bse,ed->bsd', mix, w_out[l]).astype(x.dtype)
        h = rmsnorm(x, mlp_norm[l])
        u = jnp.square(jax.nn.relu(jnp.einsum('bsd,df->bsf', h, w_up[l])))
        x = x + jnp.einsum('bsf,fd->bsd', u, w_down[l]).astype(x.dtype)
    return rmsnorm(x, final_norm)


_drawn_inputs = setup_inputs


def setup_inputs(seed=0):
    import zlib

    import numpy as np

    out = dict(_drawn_inputs(seed))
    spreads = {}
    factors = {'sb_norm': 4.692,
     'swa_norm': 4.351,
     'sinks': 6.128,
     'mlp_norm': 2.934,
     'final_norm': 2.931}
    for name, (base, spread) in spreads.items():
        noise = np.random.default_rng([zlib.crc32(name.encode()), seed]).standard_normal(out[name].shape)
        drawn = base * np.exp(spread * noise) if base else spread * noise
        out[name] = jnp.asarray(drawn.astype(out[name].dtype))
    for name, factor in factors.items():
        out[name] = (out[name] * factor).astype(out[name].dtype)
    return out
```

```python
from contextlib import ExitStack

import numpy as np

import concourse.bass as bass
from concourse import mybir

F32 = mybir.dt.float32
F32R = mybir.dt.float32r
I32 = mybir.dt.int32
ALU = mybir.AluOpType
ACT = mybir.ActivationFunctionType
AX = mybir.AxisListType

P = 128
DM = 1024
T = 512
DEPTH = 2
GROUP_ORDER = (0, 2, 1, 3)
DH = 64
SB_HEADS, SWA_HEADS, KV_HEADS = 8, 8, 2
GROUP = SWA_HEADS // KV_HEADS
D_FF = 4 * DM
EPS = 1e-6
NEG = -1e30
THETA = 10000.0
KC = DM // P
NB = T // P
SCALE = DH ** -0.5

IN_TILES = 18
OUT_TILES = KC
QUARTERS = 4
PACKS = IN_TILES + OUT_TILES + QUARTERS * 2 * KC
OUT_AT = IN_TILES
MLP_AT = IN_TILES + OUT_TILES
SPLIT_SLOTS = 4
RAW_SLOTS = 2
GAINS = KC + KC + KC

PAIR_TILES = lambda p: [("sbq", p), ("sbk", p), ("sbv", p)]
TILES = ([("swk", 0), ("swv", 0), ("swq", 0), ("swq", 1)] + PAIR_TILES(0) + PAIR_TILES(1)
         + [("swq", 2), ("swq", 3)] + PAIR_TILES(2) + PAIR_TILES(3))
COLUMN_BLOCK = {"sbq": 0, "sbk": 4, "sbv": 8, "swq": 12, "swk": 16, "swv": 17}

Z_AT = {0: 0, 1: 512, 3: 896, 2: 1024}
Z_LEN = {j: T - P * j for j in range(NB)}
Z_ALL = sum(Z_LEN.values())


def attention_steps():
    steps = []
    tile = iter(range(IN_TILES))

    def dense(n):
        return [next(tile) for _ in range(n)]

    def leave(t):
        out = [("TE", t)]
        if TILES[t][0] in ("sbv", "swv"):
            out += [("VT", t), ("VTE", t)]
        return out

    for t in dense(4):
        steps += [("T", t)] + leave(t)
    q, k, v = dense(3)
    for s, t in ((0, q), (1, k)):
        steps += [("WS", s), ("WS_MASK", s), ("T", t), ("WS_MAX", s), ("WS_EXP", s),
                  ("WS_NORM", s), ("WT", s), ("TE", t), ("WTE", s), ("WA", s), ("WAE", s)]
    steps += [("T", v)] + leave(v)
    plan = {0: (2, 2), 1: (3, 2), 2: (None, 2), 3: (4, 2), 4: (5, 1), 5: (6, 2), 6: (7, 0), 7: (None, 0)}
    for c in range(SB_HEADS):
        s, n = plan[c]
        last = plan[c - 1][0] if c else None
        t = dense(n)
        W = lambda *names: [(x, s) for x in names] if s is not None else []
        steps += W("WS") + [("BS", c)] + W("WS_MASK") + [("BS_LN", c)]
        steps += W("WS_MAX", "WS_EXP") + [("BS_SP", c)] + W("WS_NORM") + [("BS_HI", c), ("BS_LO", c)]
        if t:
            steps += [("T", t[0])]
        if c:
            steps += [("BA", c - 1)]
        if last is not None:
            steps += [("WA", last)]
        steps += W("WT")
        if n > 1:
            steps += [("T", t[1])]
        if t:
            steps += [("TE", t[0])]
        if c:
            steps += [("BAE", c - 1)]
        if last is not None:
            steps += [("WAE", last)]
        steps += W("WTE")
        if t:
            steps += leave(t[0])[1:]
        steps += [("BX", c), ("BXE", c)]
        if n > 1:
            steps += leave(t[1])
    steps += [("BA", SB_HEADS - 1), ("BAE", SB_HEADS - 1)]
    return steps


STEPS = attention_steps()


def numbered(*kinds):
    return {s: n for n, s in enumerate(x for x in STEPS if x[0] in kinds)}


W_USE = {s: n + 1 for s, n in numbered("WS", "WT", "VT").items()}
W_NORM = {"attention": 0, "swa": len(W_USE) + 1, "sb": len(W_USE) + 2, "mlp": len(W_USE) + 3}
W_USES = len(W_USE) + 4
O_USE = numbered("BA", "WA")
O_USES = len(O_USE)
QK_USE = {s[1]: n for n, s in enumerate(x for x in STEPS if x[0] == "TE" and TILES[x[1]][0][2] != "v")}
QK_USES = len(QK_USE)
V_USE = {s[1]: n for s, n in numbered("VTE").items()}
V_USES = len(V_USE)
SWA_STEPS = KV_HEADS * NB
TILE_OF = {kind: t for t, kind in enumerate(TILES)}
NORMS = 4
CREDIT = SPLIT_SLOTS
MIX_ORDER = (4, 5, 6, 7, 0, 1, 2, 3)

TWO_PI = 2 * np.pi
ROUND = 1.5 * 2.0 ** 23
PI_BELOW = 3.1415925


def pieces(value, bits, n):
    out = []
    for _ in range(n):
        unit = 2.0 ** (np.floor(np.log2(abs(value))) - bits + 1)
        out.append(float(np.round(value / unit) * unit))
        value -= out[-1]
    return out


TWO_PI_PARTS = pieces(TWO_PI, 12, 3)


def slot_of(p):
    return p % SPLIT_SLOTS


def build(nc, x_in, positions, weights, gains_in, sinks_in, inv_freq_in, out):
    with ExitStack() as ctx:
        def sb(name, shape, dtype=F32):
            return ctx.enter_context(nc.sbuf_tensor(name, shape, dtype))

        def sem(name):
            return ctx.enter_context(nc.semaphore(name))

        Z3 = ctx.enter_context(nc.psum_tensor("Z", [P, 3, T], F32))
        O = ctx.enter_context(nc.psum_tensor("O", [P, T], F32))
        D = ctx.enter_context(nc.psum_tensor("D", [P, 2, T], F32))
        W = ctx.enter_context(nc.psum_tensor("W", [P, 2, T], F32))
        Z = Z3[:, :, :].rearrange("p a b -> p (a b)")

        x = sb("x", [P, KC, T])
        xg = sb("xg", [P, 2, KC, T], F32R)
        shared = sb("shared", [P, 2 * KC * T], F32R)
        raw = sb("raw", [P, RAW_SLOTS, KC, P])
        w = sb("w", [P, SPLIT_SLOTS, 2, KC, P], F32R)
        work = sb("work", [P, Z_ALL])
        sp = sb("sp", [P, 2, Z_ALL], F32R)
        at = sb("at", [P, 2, Z_ALL], F32R)
        kvd = sb("kvd", [P, KV_HEADS, 2, T], F32R)
        vsw = sb("vsw", [P, NB, KV_HEADS, 2 * DH], F32R)
        probs = sb("probs", [P, GROUP, 2 * P])
        pt = sb("pt", [P, 2, 2, T], F32R)
        o = sb("o", [P, KC, T])
        cos = sb("cos", [P, T])
        sin = sb("sin", [P, T])
        kf = sb("kf", [P, 2, T])
        rms = sb("rms", [P, T])
        acc = sb("acc", [P, 2, T])
        other = sb("other", [P, T])
        ident = sb("ident", [P, P])
        ones = sb("ones", [P, P])
        ident_r = sb("ident_r", [P, P], F32R)
        minus_tri = sb("minus_tri", [P, P], F32R)
        minus_one = sb("minus_one", [P, P], F32R)
        strict = sb("strict", [P, P], F32R)
        band = sb("band", [P, 2 * P])
        gains = sb("gains", [P, GAINS * DEPTH + KC])
        sinks = sb("sinks", [P, DEPTH * SWA_HEADS])
        inv_freq = sb("inv_freq", [P, 1])
        small = sb("small", [P, 6, GROUP])

        mix = shared[:, :].rearrange("p (h c t) -> p h c t", h=2, c=KC)
        u = mix
        qk = shared[:, 0:8 * T].rearrange("p (s f t) -> p s f t", s=2, f=4)
        vst = shared[:, 8 * T:12 * T].rearrange("p (s j a d) -> p s j a d", s=2, j=NB, a=2)
        qsw = shared[:, 12 * T:16 * T].rearrange("p (j f t) -> p j f t", j=2, f=2)
        rms2 = probs[:, :, :].rearrange("p a b -> p (a b)")[:, 0:T]
        relu = [o[:, 0, :], o[:, 1, :]]
        w_scores = W[:, :, :].rearrange("p b (i k) -> p (b i) k", i=2)
        w_heads = W[:, 0, :].rearrange("p (m d) -> p m d", d=DH)

        def v_part(kind, j, f):
            heads = vsw[:, :, :, :] if kind == "swv" else vst[:, j % 2]
            return heads.rearrange("p j a d -> p (j a) d")[:, :, f * DH:(f + 1) * DH]

        def o_heads(buf, h, start=None):
            start = h * DH if start is None else start
            return buf[start:start + DH, :].rearrange("p (i t) -> p i t", t=P)[:, 2 * h:2 * h + 2, :]

        work0, work1 = work[:, 0:T], work[:, T:2 * T]
        rope0, rope1 = o[:, 2, :], o[:, 3, :]
        posi = work[:, 0:T].bitcast(I32)

        raw_in = [sem(f"raw_in{i}") for i in range(RAW_SLOTS)]
        x_in_sem, const_in, out_stored = sem("x_loaded"), sem("const_loaded"), sem("out_stored")
        tile_done, w_full, z_full, zx_full, o_full = map(sem, ("tile_done", "w_full", "z_full", "zx_full", "o_full"))
        (w_hi, kf_hi, v_hi, sb_ln, sb_hi, z_drained, sb_ahi, swa_exp, pt_hi, o_moved, n_exp, m_hi, x_hi,
         mlp_relu, mlp_hi, trig) = map(sem, (
             "w_hi", "kf_hi", "v_hi", "sb_ln", "sb_hi", "z_drained", "sb_ahi", "swa_exp", "pt_hi", "o_moved",
             "n_exp", "m_hi", "x_hi", "mlp_relu", "mlp_hi", "trig"))
        (d_drained, kf_full, qk_ready, v_ready, w_drained, sb_sp, sb_split, swa_max, swa_p, pt_ready,
         o_drained, m_full, m_ready, x_full, xg_ready, acc_ready, mlp_sq, u_ready, angle, y_ready) = map(sem, (
             "d_drained", "kf_full", "qk_ready", "v_ready", "w_drained", "sb_sp", "sb_split",
             "swa_max", "swa_p", "pt_ready", "o_drained", "m_full", "m_ready", "x_full", "xg_ready",
             "acc_ready", "mlp_sq", "u_ready", "angle", "y_ready"))
        w_ready, sb_alo, masks = sem("w_ready"), sem("sb_alo"), sem("masks")

        x_dram = x_in.rearrange("(c p) t -> p c t", p=P)
        out_dram = out.rearrange("(c p) t -> p c t", p=P)
        block = ctx.enter_context(nc.Block())

        @block.sync
        def _(sp_):
            sp_.dma_start(posi, positions.partition_broadcast(P)).then_inc(const_in, 16)
            sp_.dma_start(inv_freq[:, :], inv_freq_in).then_inc(const_in, 16)
            sp_.dma_start(gains[:, :], gains_in).then_inc(const_in, 16)
            sp_.dma_start(sinks[:, :], sinks_in.partition_broadcast(P)).then_inc(const_in, 16)
            for n in range(RAW_SLOTS):
                sp_.dma_start(raw[:, n], weights[n]).then_inc(raw_in[n], 16)
            with sp_.Fori(1, PACKS * DEPTH // RAW_SLOTS) as i:
                for n in range(RAW_SLOTS):
                    sp_.wait_ge(w_ready, (i - 1) * RAW_SLOTS + n + 1)
                    sp_.dma_start(raw[:, n], weights[bass.ds(i * RAW_SLOTS + n, 1)].rearrange("a p k -> p (a k)")
                                  ).then_inc(raw_in[n], 16)
            sp_.wait_ge(w_ready, PACKS * DEPTH - RAW_SLOTS + 1)
            sp_.dma_start(raw[:, 0], weights[PACKS * DEPTH]).then_inc(raw_in[0], 16)
            for c in range(KC):
                sp_.wait_ge(y_ready, c + 1)
                sp_.dma_start(out_dram[:, c, :], o[:, c, :]).then_inc(out_stored, 16)
            sp_.wait_ge(out_stored, 16 * KC)

        @block.tensor
        def _(pe):
            def dense(n, p, rhs, ready=None, order=tuple(range(KC))):
                pe.wait_ge(w_ready, n + 1)
                pe.wait_ge(d_drained, n + 1)
                slot, bank = slot_of(p), D[:, p % 2, :]
                for i, c in enumerate(order):
                    if ready is not None:
                        ready(i)
                    pe.matmul(bank, w[:, slot, 0, i], rhs[:, 0, c], start=i == 0, stop=False)
                    pe.matmul(bank, w[:, slot, 0, i], rhs[:, 1, c], start=False, stop=False)
                    mm = pe.matmul(bank, w[:, slot, 1, i], rhs[:, 0, c], start=False, stop=i == KC - 1)
                mm.then_inc(tile_done, 1)

            def norm(use, ready, which):
                pe.wait_ge(acc_ready, ready)
                pe.wait_ge(w_drained, use + 1)
                pe.matmul(W[:, 0, :], ones[:, :], acc[:, which, :], start=True, stop=True).then_inc(w_full, 1)

            pe.sem_inc(tile_done, CREDIT)
            pe.wait_ge(masks, 5)
            with pe.Fori(0, DEPTH) as l:
                norm(l * W_USES + W_NORM["attention"], l * NORMS + 1, 0)
                for step, n in STEPS:
                    if step == "T":
                        def ready(i):
                            pe.wait_ge(xg_ready, l * 2 * KC + i + 1)
                        dense(l * PACKS + n, n, xg, ready if n == 0 else None)
                    elif step == "VT":
                        pe.wait_ge(kf_full, l * IN_TILES + n + 1)
                        pe.wait_ge(w_drained, l * W_USES + W_USE[step, n] + 1)
                        for j in range(NB):
                            mm = pe.transpose(W[:, 0, j * P:(j + 1) * P], kf[:, n % 2, j * P:(j + 1) * P], ident[:, :])
                        mm.then_inc(w_full, 1)
                    elif step == "WS":
                        g, b = divmod(n, NB)
                        pe.wait_ge(w_drained, l * W_USES + W_USE[step, n] + 1)
                        if b == 0:
                            pe.wait_ge(qk_ready, l * QK_USES + QK_USE[TILE_OF["swq", 2 * g + 1]] + 1)
                        k0, at0 = (b - 1, 0) if b else (0, P)
                        for i in range(GROUP):
                            half = slice(i % 2 * DH, i % 2 * DH + DH)
                            dst = W[:, i % 2, i // 2 * 2 * P + at0:(i // 2 + 1) * 2 * P]
                            for f, (ql, kl) in enumerate(((0, 0), (0, 1), (1, 0))):
                                mm = pe.matmul(dst, qsw[half, i // 2, ql, b * P:(b + 1) * P],
                                               kvd[half, g, kl, k0 * P:(b + 1) * P], start=f == 0, stop=f == 2)
                        mm.then_inc(w_full, 1)
                    elif step == "WT":
                        g, b = divmod(n, NB)
                        pe.wait_ge(swa_p, l * SWA_STEPS + n + 1)
                        pe.wait_ge(w_drained, l * W_USES + W_USE[step, n] + 1)
                        for kb in (0, 1) if b else (1,):
                            for i in range(GROUP):
                                mm = pe.transpose(W[:, kb, i * P:(i + 1) * P], probs[:, i, kb * P:(kb + 1) * P],
                                                  ident[:, :])
                        mm.then_inc(w_full, 1)
                    elif step == "WA":
                        g, b = divmod(n, NB)
                        pe.wait_ge(pt_ready, l * SWA_STEPS + n + 1)
                        pe.wait_ge(o_drained, l * O_USES + O_USE[step, n] + 1)
                        if n == 0:
                            pe.wait_ge(v_ready, l * V_USES + V_USE[TILE_OF["swv", 0]] + 1)
                        kbs = (0, 1) if b else (1,)
                        for kb in kbs:
                            for f in range(2):
                                mm = pe.matmul(O[:, :], vsw[:, b - 1 + kb, g, :], pt[:, f, kb, :],
                                               start=kb == kbs[0] and f == 0, stop=kb == 1 and f == 1)
                        mm.then_inc(o_full, 1)
                    elif step == "BS":
                        par, half = n // 2 % 2, slice(n % 2 * DH, n % 2 * DH + DH)
                        pe.wait_ge(z_drained, l * SB_HEADS + n + 1)
                        if n % 2 == 0:
                            pe.wait_ge(qk_ready, l * QK_USES + QK_USE[TILE_OF["sbk", n // 2]] + 1)
                        for j in (0, 1, 3, 2):
                            dst = Z[:, Z_AT[j]:Z_AT[j] + Z_LEN[j]]
                            for f, (kl, ql) in enumerate(((2, 0), (2, 1), (3, 0))):
                                pe.matmul(dst, qk[half, par, kl, j * P:(j + 1) * P], qk[half, par, ql, j * P:T],
                                          start=f == 0 and j != 3, stop=False, skip_group_check=True)
                            mm = pe.matmul(Z[:, Z_AT[j]:Z_AT[j] + P], ident_r[:, :], strict[:, :],
                                           start=False, stop=True, skip_group_check=True)
                        mm.then_inc(z_full, 1)
                    elif step == "BX":
                        pe.wait_ge(sb_split, l * SB_HEADS + n + 1)
                        for j in (0, 1, 3, 2):
                            for jj in range(j, NB):
                                at0 = Z_AT[j] + P * (jj - j)
                                for f in range(2):
                                    mm = pe.matmul(Z[:, at0:Z_AT[j] + Z_LEN[j]],
                                                   (minus_tri if jj == j else minus_one)[:, :],
                                                   sp[:, f, Z_AT[jj]:Z_AT[jj] + Z_LEN[jj]],
                                                   start=False, stop=jj == NB - 1 and f == 1, skip_group_check=True)
                        mm.then_inc(zx_full, 1)
                    elif step == "BA":
                        pe.wait_ge(sb_alo, l * SB_HEADS + n + 1)
                        pe.wait_ge(o_drained, l * O_USES + O_USE[step, n] + 1)
                        if n % 2 == 0:
                            pe.wait_ge(v_ready, l * V_USES + V_USE[TILE_OF["sbv", n // 2]] + 1)
                        for j in range(NB):
                            for f in range(2):
                                mm = pe.matmul(O[:, j * P:T], vst[:, n // 2 % 2, j, n % 2, :],
                                               at[:, f, Z_AT[j]:Z_AT[j] + Z_LEN[j]],
                                               start=j == 0 and f == 0, stop=j == NB - 1 and f == 1)
                        mm.then_inc(o_full, 1)
                norm(l * W_USES + W_NORM["swa"], l * NORMS + 2, 0)
                norm(l * W_USES + W_NORM["sb"], l * NORMS + 3, 1)
                for d in range(OUT_TILES):
                    def ready(i):
                        pe.wait_ge(m_ready, l * KC + i + 1)
                    dense(l * PACKS + OUT_AT + d, OUT_AT + d, mix, ready if d == 0 else None, MIX_ORDER)
                norm(l * W_USES + W_NORM["mlp"], l * NORMS + 4, 0)
                with pe.Fori(0, QUARTERS) as q:
                    for c in range(KC):
                        def ready(i):
                            pe.wait_ge(xg_ready, l * 2 * KC + KC + i + 1)
                        p = MLP_AT + c
                        dense(l * PACKS + q * 2 * KC + p, p, xg, ready if c == 0 else None)
                    for d in range(KC):
                        def ready(i):
                            pe.wait_ge(u_ready, l * QUARTERS * KC + q * KC + i + 1)
                        p = MLP_AT + KC + d
                        dense(l * PACKS + q * 2 * KC + p, p, u, ready if d == 0 else None)
            norm(DEPTH * W_USES, DEPTH * NORMS + 1, 0)

        @block.scalar
        def _(act):
            def split_weights(p, arrived, free):
                act.wait_ge(raw_in[p % 2], arrived)
                act.wait_ge(tile_done, free)
                act.activation(w[:, slot_of(p), 0], raw[:, p % 2], ACT.Identity).then_inc(w_hi, 1)

            def split(l, p, q=0):
                prior = SPLIT_SLOTS if 1 < p else 2
                n = q * 2 * KC + p
                arrived = l * (PACKS // 2 * 16) + q * (KC * 16) + (p // 2 + 1) * 16
                split_weights(p, arrived, l * PACKS + n + 1 - prior + CREDIT)

            def norm(use):
                act.wait_ge(w_drained, use + 2)
                act.activation(work1, work0, ACT.Ln)
                act.drain()
                act.activation(work1, work1, ACT.Exp, scale=-0.5).then_inc(n_exp, 1)

            def chunk_hi(count, c, gain):
                act.wait_ge(x_full, count + 1)
                act.activation(xg[:, 0, c], x[:, c], ACT.Identity, scale=gain).then_inc(x_hi, 1)

            for c in range(KC):
                act.dma_start(x[:, c], x_dram[:, c]).then_inc(x_in_sem, 16)
            act.wait_ge(angle, 1)
            act.activation(sin[:, :], work0, ACT.Sin)
            act.activation(cos[:, :], kf[:, 0], ACT.Sin).then_inc(trig, 1)
            act.preload_act_table_set("natural_log_exp_and_others")
            act.wait_ge(const_in, 64)
            act.sem_inc(z_drained, 1)
            act.wait_ge(raw_in[0], 16)
            act.activation(w[:, 0, 0], raw[:, 0], ACT.Identity).then_inc(w_hi, 1)
            for c in range(KC):
                act.wait_ge(x_in_sem, 16 * KC)
                act.activation(xg[:, 0, c], x[:, c], ACT.Identity, scale=gains[:, c:c + 1]).then_inc(x_hi, 1)
            with act.Fori(0, DEPTH) as l:
                split(l, 1)
                split(l, 2)
                norm(l * W_USES + W_NORM["attention"])
                for step, n in STEPS:
                    if step == "T":
                        split(l, n + 3)
                    elif step == "TE" and TILES[n][0][2] != "v":
                        kind, j = TILES[n]
                        act.wait_ge(kf_full, l * IN_TILES + n + 1)
                        if kind == "swk":
                            for g in range(KV_HEADS):
                                for h in range(2):
                                    last = act.activation(kvd[h * DH:h * DH + DH, g, 0], kf[g * DH:g * DH + DH, n % 2],
                                                          ACT.Identity)
                        elif kind == "swq":
                            last = act.activation(qsw[:, j % 2, 0], kf[:, n % 2], ACT.Identity)
                        else:
                            last = act.activation(qk[:, j % 2, 0 if kind == "sbq" else 2], kf[:, n % 2], ACT.Identity)
                        last.then_inc(kf_hi, 1)
                    elif step == "VTE":
                        act.wait_ge(w_full, l * W_USES + W_USE["VT", n] + 1)
                        kind, j = TILES[n]
                        act.activation(v_part(kind, j, 0), w_heads, ACT.Identity).then_inc(v_hi, 1)
                    elif step == "BS_LN":
                        act.wait_ge(z_full, l * SB_HEADS + n + 1)
                        if n:
                            act.wait_ge(sb_alo, l * SB_HEADS + n)
                        act.activation(work[:, :], Z[:, 0:Z_ALL], ACT.Abs)
                        act.drain()
                        act.activation(work[:, :], work[:, :], ACT.Exp, scale=-1.0)
                        act.drain()
                        act.activation(work[:, :], work[:, :], ACT.Ln, bias=1.0).then_inc(sb_ln, 1)
                    elif step == "BS_HI":
                        act.wait_ge(sb_sp, l * SB_HEADS + n + 1)
                        act.activation(sp[:, 0], work[:, :], ACT.Identity).then_inc(sb_hi, 1)
                    elif step == "BXE":
                        act.wait_ge(zx_full, l * SB_HEADS + n + 1)
                        act.activation(work[:, :], Z[:, 0:Z_ALL], ACT.Exp).then_inc(z_drained, 1)
                        act.drain()
                        if n:
                            act.wait_ge(o_full, l * O_USES + O_USE["BA", n - 1] + 1)
                        act.activation(at[:, 0], work[:, :], ACT.Identity).then_inc(sb_ahi, 1)
                    elif step == "BAE":
                        act.wait_ge(o_full, l * O_USES + O_USE["BA", n] + 1)
                        a, b = n % 2 * DH, (1 - n % 2) * DH
                        act.activation(other[a:a + DH, :], O[b:b + DH, :], ACT.Identity).then_inc(o_moved, 1)
                    elif step == "WS_EXP":
                        g, b = divmod(n, NB)
                        act.wait_ge(swa_max, l * SWA_STEPS + n + 1)
                        at0 = 0 if b else P
                        for i in range(GROUP):
                            act.activation(probs[:, i, at0:], probs[:, i, at0:], ACT.Exp, bias=small[:, 0, i:i + 1],
                                           accum_out=small[:, 3, i:i + 1])
                        act.activation(small[:, 2, :], small[:, 1, :], ACT.Exp).then_inc(swa_exp, 1)
                    elif step == "WTE":
                        g, b = divmod(n, NB)
                        act.wait_ge(w_full, l * W_USES + W_USE["WT", n] + 1)
                        kb = 0 if b else 1
                        if n:
                            act.wait_ge(o_full, l * O_USES + O_USE["WA", n - 1] + 1)
                        act.activation(pt[:, 0, kb:], W[:, kb:], ACT.Identity).then_inc(pt_hi, 1)
                    elif step == "WAE":
                        act.wait_ge(o_full, l * O_USES + O_USE["WA", n] + 1)
                        act.activation(o_heads(other, 0), o_heads(O, 0, DH), ACT.Identity)
                        act.activation(o_heads(other, 1), o_heads(O, 1, 0), ACT.Identity).then_inc(o_moved, 1)
                for k, which in ((1, "swa"), (2, "sb")):
                    norm(l * W_USES + W_NORM[which])
                    for i in range(NB):
                        e = MIX_ORDER[(k - 1) * NB + i]
                        act.wait_ge(m_full, l * KC + (k - 1) * NB + i + 1)
                        act.activation(mix[:, 0, e], kf[:, i % 2], ACT.Identity).then_inc(m_hi, 1)
                for d in range(OUT_TILES):
                    if d >= 2:
                        split(l, OUT_AT + d + 1)
                    chunk_hi(l * 2 * KC + d, d, gains[:, bass.ds(l * GAINS + 2 * KC + d, 1)])
                norm(l * W_USES + W_NORM["mlp"])

                def quarter(q, last):
                    for c in range(KC):
                        split(l, MLP_AT + c + 1, q)
                        act.wait_ge(tile_done, l * PACKS + q * 2 * KC + MLP_AT + c + 1 + CREDIT)
                        act.activation(relu[c % 2], D[:, (MLP_AT + c) % 2], ACT.Relu).then_inc(mlp_relu, 1)
                        act.wait_ge(mlp_sq, l * QUARTERS * KC + q * KC + c + 1)
                        act.activation(u[:, 0, c], kf[:, c % 2], ACT.Identity).then_inc(mlp_hi, 1)
                    for d in range(KC):
                        if last and d == KC - 1:
                            split_weights(0, l * (PACKS // 2 * 16) + (PACKS // 2 + 1) * 16,
                                          l * PACKS + PACKS - 1 + CREDIT)
                        else:
                            split(l, MLP_AT + KC + d + 1, q)
                        if last:
                            chunk_hi(l * 2 * KC + KC + d, d, gains[:, bass.ds(l * GAINS + GAINS + d, 1)])

                with act.Fori(0, QUARTERS - 1) as q:
                    quarter(q, False)
                quarter(QUARTERS - 1, True)
            norm(DEPTH * W_USES)

        @block.gpsimd
        def _(pool):
            def split(n, p):
                pool.wait_ge(w_hi, n + 1)
                slot = slot_of(p)
                pool.tensor_tensor(w[:, slot, 1], raw[:, p % 2], w[:, slot, 0].bitcast(F32), ALU.subtract
                                   ).then_inc(w_ready, 1)

            def constant(dst, value, fill, compare, base, step, channel):
                pool.memset(dst, value)
                pool.drain()
                pool.affine_select(out=dst, in_=dst, compare_op=compare, fill=fill, base=base,
                                   pattern=[[step, dst.shape[1]]], channel_multiplier=channel)
                pool.drain()

            constant(ident[:, :], 0.0, 1.0, ALU.not_equal, 0, -1, 1)
            pool.memset(ones[:, :], 1.0)
            tri, row, low = (probs[:, i, 0:P] for i in range(3))
            constant(tri, -1.0, 0.0, ALU.is_ge, 0, -1, 1)
            constant(low, 0.0, NEG, ALU.is_gt, 0, 1, -1)
            pool.memset(row, -1.0)
            constant(band[:, :], 0.0, NEG, ALU.is_ge, P, -1, 1)
            pool.affine_select(out=band[:, :], in_=band[:, :], compare_op=ALU.is_gt, fill=NEG, base=0,
                               pattern=[[1, 2 * P]], channel_multiplier=-1).then_inc(masks, 1)
            pool.drain()
            for dst, src in ((ident_r, ident[:, :]), (minus_tri, tri), (minus_one, row), (strict, low)):
                pool.tensor_copy(dst[:, :], src).then_inc(masks, 1)
            split(0, 0)
            with pool.Fori(0, DEPTH) as l:
                split(l * PACKS + 1, 1)
                split(l * PACKS + 2, 2)
                for step, n in STEPS:
                    if step == "T":
                        split(l * PACKS + n + 3, n + 3)
                    elif step == "BXE":
                        pool.wait_ge(sb_ahi, l * SB_HEADS + n + 1)
                        pool.tensor_tensor(at[:, 1], work[:, :], at[:, 0].bitcast(F32), ALU.subtract
                                           ).then_inc(sb_alo, 1)
                for d in range(2, OUT_TILES):
                    split(l * PACKS + OUT_AT + d + 1, OUT_AT + d + 1)
                with pool.Fori(0, QUARTERS - 1) as q:
                    for p in range(MLP_AT + 1, MLP_AT + 2 * KC + 1):
                        split(l * PACKS + q * 2 * KC + p, p)
                for p in range(MLP_AT + 1, MLP_AT + 2 * KC):
                    split(l * PACKS + (QUARTERS - 1) * 2 * KC + p, p)
                split(l * PACKS + PACKS, 0)

        @block.vector
        def _(dve):
            def norm(use, count, width, dst):
                dve.wait_ge(w_full, use + 1)
                dve.tensor_scalar(work0, W[:, 0, :], 1.0 / width, EPS, ALU.mult, ALU.add).then_inc(w_drained, 1)
                dve.wait_ge(n_exp, count + 1)
                dve.scalar_tensor_tensor(dst, work0, -0.5, work1, ALU.mult, ALU.mult)
                dve.drain()
                dve.tensor_tensor(dst, dst, work1, ALU.mult)
                dve.drain()
                dve.scalar_tensor_tensor(dst, dst, 1.5, work1, ALU.add, ALU.mult)
                dve.drain()

            def squares(src, which, first, final, tmp):
                if first:
                    last = dve.tensor_tensor(acc[:, which], src, src, ALU.mult)
                else:
                    dve.tensor_tensor(tmp, src, src, ALU.mult)
                    dve.drain()
                    last = dve.tensor_tensor(acc[:, which], acc[:, which], tmp, ALU.add)
                if final:
                    last.then_inc(acc_ready, 1)
                dve.drain()

            def chunk_lo(count, c, gain):
                dve.wait_ge(x_hi, count + 1)
                dve.scalar_tensor_tensor(xg[:, 1, c], x[:, c], gain, xg[:, 0, c].bitcast(F32), ALU.mult,
                                         ALU.subtract).then_inc(xg_ready, 1)
                squares(x[:, c], 0, c == 0, c == KC - 1, kf[:, 1])

            def rope(n):
                src = kf[:, n % 2]
                dve.tensor_tensor(rope0, src, cos[:, :], ALU.mult)
                for a in range(4):
                    b = a ^ 1
                    dve.tensor_tensor(rope1[b * 32:b * 32 + 32], kf[a * 32:a * 32 + 32, n % 2], sin[a * 32:a * 32 + 32, :],
                                      ALU.mult)
                dve.drain()
                return dve.tensor_tensor(src, rope0, rope1, ALU.add)

            dve.wait_ge(const_in, 64)
            dve.tensor_copy(kf[:, 0], posi)
            dve.drain()
            dve.tensor_scalar(work1, kf[:, 0], inv_freq[:, 0:1], None, ALU.mult)
            dve.drain()
            dve.tensor_scalar(kf[:, 0], work1, 1.0 / TWO_PI, ROUND, ALU.mult, ALU.add)
            dve.drain()
            dve.tensor_scalar(kf[:, 0], kf[:, 0], ROUND, None, ALU.subtract)
            dve.drain()
            dve.tensor_scalar(kf[:, 1], kf[:, 0], ROUND * 2048, None, ALU.add)
            dve.drain()
            dve.tensor_scalar(kf[:, 1], kf[:, 1], ROUND * 2048, None, ALU.subtract)
            dve.drain()
            dve.tensor_tensor(kf[:, 0], kf[:, 0], kf[:, 1], ALU.subtract)
            dve.drain()
            for part in TWO_PI_PARTS:
                for k in (1, 0):
                    dve.scalar_tensor_tensor(work1, kf[:, k], -part, work1, ALU.mult, ALU.add)
                    dve.drain()
            dve.tensor_scalar(work0, work1, PI_BELOW, -PI_BELOW, ALU.min, ALU.max)
            dve.drain()
            dve.scalar_tensor_tensor(kf[:, 0], work0, -1.0, work0, ALU.mult, ALU.min)
            dve.drain()
            dve.tensor_scalar(kf[:, 0], kf[:, 0], float(np.float32(np.pi / 2)), None, ALU.add).then_inc(angle, 1)
            dve.wait_ge(trig, 1)
            for a in (1, 3):
                dve.tensor_scalar(sin[a * 32:a * 32 + 32, :], sin[a * 32:a * 32 + 32, :], -1.0, None, ALU.mult)
            dve.drain()
            dve.wait_ge(masks, 5)
            dve.sem_inc(d_drained, 2)
            dve.sem_inc(w_drained, 1)
            dve.sem_inc(o_drained, 1)
            for c in range(KC):
                chunk_lo(c, c, gains[:, c:c + 1])

            with dve.Fori(0, DEPTH) as l:
                norm(l * W_USES + W_NORM["attention"], l * NORMS, DM, rms[:, :])
                for step, n in STEPS:
                    if step == "TE":
                        kind, j = TILES[n]
                        dve.wait_ge(tile_done, l * PACKS + n + 1 + CREDIT)
                        scale = SCALE if kind in ("sbq", "swq") else 1.0
                        last = dve.scalar_tensor_tensor(kf[:, n % 2], D[:, n % 2], scale, rms[:, :], ALU.mult, ALU.mult)
                        last.then_inc(d_drained, 1)
                        if kind in ("swk", "swq"):
                            dve.drain()
                            rope(n).then_inc(kf_full, 1)
                        else:
                            dve.drain().then_inc(kf_full, 1)
                        if kind[2] != "v":
                            dve.wait_ge(kf_hi, l * QK_USES + QK_USE[n] + 1)
                            if kind == "swk":
                                for g in range(KV_HEADS):
                                    for h in range(2):
                                        rows = slice(g * DH, g * DH + DH)
                                        last = dve.tensor_tensor(kvd[h * DH:h * DH + DH, g, 1], kf[rows, n % 2],
                                                                 kvd[rows, g, 0].bitcast(F32), ALU.subtract)
                            else:
                                f = {"swq": (qsw, j % 2, 0), "sbq": (qk, j % 2, 0), "sbk": (qk, j % 2, 2)}[kind]
                                last = dve.tensor_tensor(f[0][:, f[1], f[2] + 1], kf[:, n % 2],
                                                         f[0][:, f[1], f[2]].bitcast(F32), ALU.subtract)
                            last.then_inc(qk_ready, 1)
                    elif step == "VTE":
                        dve.wait_ge(v_hi, l * V_USES + V_USE[n] + 1)
                        kind, j = TILES[n]
                        dve.tensor_tensor(v_part(kind, j, 1), w_heads, v_part(kind, j, 0).bitcast(F32), ALU.subtract
                                          ).then_inc(v_ready, 1)
                        dve.drain().then_inc(w_drained, 1)
                    elif step == "BS_SP":
                        dve.wait_ge(sb_ln, l * SB_HEADS + n + 1)
                        dve.scalar_tensor_tensor(work[:, :], Z[:, 0:Z_ALL], 0.0, work[:, :], ALU.max, ALU.add
                                                 ).then_inc(sb_sp, 1)
                    elif step == "BS_LO":
                        dve.wait_ge(sb_hi, l * SB_HEADS + n + 1)
                        dve.tensor_tensor(sp[:, 1], work[:, :], sp[:, 0].bitcast(F32), ALU.subtract
                                          ).then_inc(sb_split, 1)
                    elif step == "BAE":
                        dve.wait_ge(o_moved, l * O_USES + O_USE["BA", n] + 1)
                        a = n % 2 * DH
                        dve.tensor_tensor(o[a:a + DH, n // 2], O[a:a + DH, :], other[a:a + DH, :], ALU.add)
                        dve.drain()
                        if n % 2:
                            squares(o[:, n // 2], 1, n == 1, n == SB_HEADS - 1, other[:, :])
                        dve.drain().then_inc(o_drained, 1)
                    elif step == "WS_MASK":
                        g, b = divmod(n, NB)
                        at0 = 0 if b else P
                        dve.wait_ge(w_full, l * W_USES + W_USE["WS", n] + 1)
                        dve.tensor_tensor(probs[:, :, at0:], w_scores[:, :, at0:],
                                          band[:, at0:].unsqueeze(1).to_broadcast([P, GROUP, 2 * P - at0]),
                                          ALU.add).then_inc(w_drained, 1)
                        dve.drain()
                    elif step == "WS_MAX":
                        g, b = divmod(n, NB)
                        at0 = 0 if b else P
                        sink = sinks[:, bass.ds(l * SWA_HEADS + g * GROUP, GROUP)]
                        dve.tensor_reduce(small[:, 5, :], probs[:, :, at0:], AX.X, ALU.max)
                        dve.drain()
                        dve.tensor_tensor(small[:, 1, :], small[:, 5, :], sink, ALU.max)
                        dve.drain()
                        dve.tensor_scalar(small[:, 0, :], small[:, 1, :], -1.0, None, ALU.mult)
                        dve.drain()
                        dve.tensor_tensor(small[:, 1, :], sink, small[:, 0, :], ALU.add).then_inc(swa_max, 1)
                    elif step == "WS_NORM":
                        g, b = divmod(n, NB)
                        at0 = 0 if b else P
                        dve.wait_ge(swa_exp, l * SWA_STEPS + n + 1)
                        dve.tensor_tensor(small[:, 4, :], small[:, 3, :], small[:, 2, :], ALU.add)
                        dve.drain()
                        dve.reciprocal(small[:, 4, :], small[:, 4, :])
                        dve.drain()
                        for i in range(GROUP):
                            last = dve.tensor_scalar(probs[:, i, at0:], probs[:, i, at0:], small[:, 4, i:i + 1], None,
                                                     ALU.mult)
                        last.then_inc(swa_p, 1)
                    elif step == "WTE":
                        g, b = divmod(n, NB)
                        kb = 0 if b else 1
                        dve.wait_ge(pt_hi, l * SWA_STEPS + n + 1)
                        dve.tensor_tensor(pt[:, 1, kb:], W[:, kb:], pt[:, 0, kb:].bitcast(F32), ALU.subtract
                                          ).then_inc(pt_ready, 1)
                        dve.drain().then_inc(w_drained, 1)
                    elif step == "WAE":
                        g, b = divmod(n, NB)
                        dve.wait_ge(o_moved, l * O_USES + O_USE["WA", n] + 1)
                        for h in range(2):
                            rows = slice(h * DH, h * DH + DH)
                            dve.tensor_tensor(o[rows, NB + 2 * g:NB + 2 * g + 2, b * P:(b + 1) * P],
                                                     o_heads(O, h), o_heads(other, h), ALU.add)
                        dve.drain()
                        if b == NB - 1:
                            for e in range(NB + 2 * g, NB + 2 * g + 2):
                                squares(o[:, e], 0, e == NB, e == KC - 1, other[:, :])
                        dve.drain().then_inc(o_drained, 1)
                for k, width, which in ((1, SWA_HEADS * DH, "swa"), (2, SB_HEADS * DH, "sb")):
                    norm(l * W_USES + W_NORM[which], l * NORMS + k, width, rms[:, :])
                    for i in range(NB):
                        e = MIX_ORDER[(k - 1) * NB + i]
                        dve.scalar_tensor_tensor(kf[:, i % 2], o[:, e], gains[:, bass.ds(l * GAINS + KC + e, 1)],
                                                 rms[:, :], ALU.mult, ALU.mult).then_inc(m_full, 1)
                        dve.wait_ge(m_hi, l * KC + (k - 1) * NB + i + 1)
                        dve.tensor_tensor(mix[:, 1, e], kf[:, i % 2], mix[:, 0, e].bitcast(F32), ALU.subtract
                                          ).then_inc(m_ready, 1)
                        dve.drain()
                for d in range(OUT_TILES):
                    dve.wait_ge(tile_done, l * PACKS + OUT_AT + d + 1 + CREDIT)
                    dve.tensor_tensor(x[:, d], D[:, (OUT_AT + d) % 2], x[:, d], ALU.add).then_inc(d_drained, 1)
                    dve.drain().then_inc(x_full, 1)
                    chunk_lo(l * 2 * KC + KC + d, d, gains[:, bass.ds(l * GAINS + 2 * KC + d, 1)])
                norm(l * W_USES + W_NORM["mlp"], l * NORMS + 3, DM, rms[:, :])
                dve.tensor_tensor(rms2, rms[:, :], rms[:, :], ALU.mult)
                dve.drain()

                def quarter(q, last):
                    for c in range(KC):
                        count = l * QUARTERS * KC + q * KC + c
                        dve.wait_ge(mlp_relu, count + 1)
                        dve.tensor_tensor(kf[:, c % 2], relu[c % 2], relu[c % 2], ALU.mult).then_inc(mlp_sq, 1)
                        dve.sem_inc(d_drained, 1)
                        dve.wait_ge(mlp_hi, count + 1)
                        dve.tensor_tensor(u[:, 1, c], kf[:, c % 2], u[:, 0, c].bitcast(F32), ALU.subtract
                                          ).then_inc(u_ready, 1)
                        dve.drain()
                    for d in range(KC):
                        p = MLP_AT + KC + d
                        dve.wait_ge(tile_done, l * PACKS + q * 2 * KC + p + 1 + CREDIT)
                        dve.tensor_tensor(kf[:, 0], D[:, p % 2], rms2, ALU.mult).then_inc(d_drained, 1)
                        dve.drain()
                        done = dve.tensor_tensor(x[:, d], x[:, d], kf[:, 0], ALU.add)
                        if last:
                            done.then_inc(x_full, 1)
                            dve.drain()
                            chunk_lo(l * 2 * KC + 2 * KC + d, d, gains[:, bass.ds(l * GAINS + GAINS + d, 1)])
                        else:
                            dve.drain()

                with dve.Fori(0, QUARTERS - 1) as q:
                    quarter(q, False)
                quarter(QUARTERS - 1, True)
            norm(DEPTH * W_USES, DEPTH * NORMS, DM, rms[:, :])
            for c in range(KC):
                dve.scalar_tensor_tensor(o[:, c], x[:, c], gains[:, DEPTH * GAINS + c:DEPTH * GAINS + c + 1], rms[:, :],
                                         ALU.mult, ALU.mult).then_inc(y_ready, 1)


def kernel(**inputs):
    import concourse.bacc as bacc
    from concourse.bass_utils import run_bass_kernel_spmd
    a = {k: np.ascontiguousarray(v) for k, v in inputs.items()}

    def packs(matrix, k0, m):
        part = matrix[k0 * P:(k0 + KC) * P, m * P:(m + 1) * P]
        return part.reshape(KC, P, P).transpose(1, 0, 2)

    order = []
    for l in range(DEPTH):
        for kind, j in TILES:
            order.append(packs(a["w_in"][l], 0, COLUMN_BLOCK[kind] + j))
        for d in range(OUT_TILES):
            order.append(packs(a["w_out"][l], 0, d)[:, list(MIX_ORDER)])
        for q in range(QUARTERS):
            for c in range(KC):
                order.append(packs(a["w_up"][l], 0, q * KC + c))
            for d in range(KC):
                order.append(packs(a["w_down"][l], q * KC, d))
    order.append(order[0])
    weights = np.stack(order).reshape(PACKS * DEPTH + 1, P, KC * P)
    gains = [a["final_norm"]]
    for l in reversed(range(DEPTH)):
        gains = [a["attn_norm"][l], a["sb_norm"][l], a["swa_norm"][l], a["mlp_norm"][l]] + gains
    gains = np.concatenate(gains).reshape(-1, P).T
    half = DH // 2
    inv_freq = np.tile((1.0 / (THETA ** (np.arange(half) * (2.0 / DH)))).astype(np.float32), P // half)[:, None]
    arrays = {
        "in_x": a["x"][0].T, "in_positions": a["positions"][None, :], "in_weights": weights, "in_gains": gains,
        "in_sinks": a["sinks"].reshape(-1, GROUP)[:, list(GROUP_ORDER)].reshape(1, -1), "in_inv_freq": inv_freq,
    }
    arrays = {k: np.ascontiguousarray(v) for k, v in arrays.items()}
    nc = bacc.Bacc("TRN2", target_bir_lowering=False, num_devices=1)
    args = [nc.dram_tensor(k, v.shape, mybir.dt.from_np(v.dtype), kind="ExternalInput").ap() for k, v in arrays.items()]
    args.append(nc.dram_tensor("out_x", (DM, T), F32, kind="ExternalOutput").ap())
    build(nc, *args)
    r = run_bass_kernel_spmd(nc, [arrays], core_ids=[0])
    return np.ascontiguousarray(r.results[0]["out_x"].T)[None]
```

```python
from contextlib import ExitStack

import numpy as np

import concourse.bass as bass
from concourse import mybir

F32 = mybir.dt.float32
F32R = mybir.dt.float32r
I32 = mybir.dt.int32
ALU = mybir.AluOpType
ACT = mybir.ActivationFunctionType
AX = mybir.AxisListType

P = 128
DM = 1024
T = 512
DEPTH = 2
DH = 64
SB_HEADS, SWA_HEADS, KV_HEADS = 8, 8, 2
SB_W, SWA_W = SB_HEADS * DH, SWA_HEADS * DH
PAIRS = SB_HEADS // 2
D_FF = 4 * DM
EPS = 1e-6
NEG = -1e30
THETA = 10000.0
KC = DM // P
NB = T // P
SCALE = DH ** -0.5

IN_TILES = 18
OUT_PACKS = KC // 2
QUARTERS = 4
SWA_OUT, SB_OUT = IN_TILES, IN_TILES + OUT_PACKS
MLP_AT = IN_TILES + 2 * OUT_PACKS
PACKS = MLP_AT + QUARTERS * 2 * KC
SPLIT_SLOTS = 4
RAW_SLOTS = 2
AHEAD = SPLIT_SLOTS - 1
GAINS = KC + KC + KC

SWA_TILE = IN_TILES
SB_TILE = SWA_TILE + KC
MLP_TILE = SB_TILE + KC
DENSE = MLP_TILE + QUARTERS * 2 * KC

PAIR_TILES = lambda p: [("sbq", p), ("sbk", p), ("sbv", p)]
TILES = (PAIR_TILES(0)
          + [("swk", 0), ("swq", 0), ("swq", 1), ("sbq", 1), ("sbk", 1), ("swv", 0), ("sbv", 1), ("sbq", 2), ("sbk", 2), ("swq", 2), ("swq", 3), ("sbv", 2)] + PAIR_TILES(3))
TILE_OF = {kind: t for t, kind in enumerate(TILES)}
COLUMN_BLOCK = {"sbq": 0, "sbk": 4, "sbv": 8, "swq": 12, "swk": 16, "swv": 17}

Z_AT = {0: 0, 1: 512, 3: 896, 2: 1024}
Z_LEN = {j: T - P * j for j in range(NB)}
Z_ALL = sum(Z_LEN.values())

ORDER = """
T0 U0 NA0 NAD0 NAE0 NAF0 CH3 TE0 TH0 T1 U1 TE1 TL0 TH1 T2 CL3 TL1 CH4 BS0 U2 T3 U3 TE2 CL4 T4 CH5 BE0 CH6
BP0 VT2 BH0 BL0 BX0 CL5 VH2 TE3 VL2 XE0 CL6 U4 TE4 XH0 TH3 CH7 T5 CL7 U5 TL3 XL0 TH4 TL4 BS1 BE1 TE5 CH8 T6
TH5 BP1 BA0 U6 BH1 TL5 WS0 T7 TE6 BL1 WK0 TH6 BX1 TL6 CL8 WM0 U7 WE0 WN0 XE1 T8 TE7 CH9 TH7 XH1 CL9 BO0 WT0
WH0 TL7 BD0 WL0 CH10 BS2 WS1 U8 WK1 WM1 XL1 T9 CL10 BE2 WE1 TE8 VT8 BP2 CH11 WN1 VH8 VL8 BA1 BO1 BD1 U9 CH12
WT1 WA0 CL11 BH2 BL2 T10 WO0 WH1 WL1 BX2 XE2 XH2 WS2 WD0 WK2 WM2 U10 MH0 BS3 TE9 ML0 XL2 CH13 VT9 WE2 VH9
VL9 T11 CL12 BA2 BE3 BO2 WN2 TE10 BP3 CL13 CH14 U11 WT2 BD2 BH3 CL14 WA1 TH10 TE11 WO1 TL10 CH15 T12 WD1 U12
WH2 TH11 BL3 BX3 WL2 MH1 CL15 WS3 TE12 WK3 CH16 XE3 XH3 TL11 XL3 T13 ML1 WM3 U13 TE13 BA3 BS4 BO3 T14 WE3
U14 WN3 CH17 BE4 TH12 BD3 WT3 WA2 T15 BP4 WO2 TL12 U15 WH3 WD2 BH4 TH13 TE14 BL4 BX4 MH2 XE4 CL16 TL13 XH4
CL17 WL3 XL4 ML2 WS4 WK4 WA3 VT14 WM4 WE4 VH14 BS5 T16 WO3 TE15 WD3 BE5 U16 MH3 WN4 VL14 WT4 WH4 BP5 WL4 T17
TH15 BH5 TL15 ML3 WS5 BL5 CH18 WK5 CH19 TE16 WM5 TH16 U17 GH0 BA4 BO4 GL0 BD4 WE5 BX5 XE5 WA4 WO4 TL16 WN5
CL18 XH5 WT5 XL5 WD4 WH5 BS6 WL5 GH1 MH4 ML4 WS6 BA5 BE6 BO5 WK6 WM6 BP6 BD5 BH6 BL6 WA5 WE6 WO5 WN6 WD5
CH20 WT6 WH6 MH5 BX6 WL6 CL19 TE17 ML5 WS7 XE6 WA6 XH6 WK7 WM7 BS7 WO6 WD6 WE7 MH6 XL6 WN7 GL1 WT7 BE7 WH7
CH21 ML6 BP7 WL7 CL20 BH7 WA7 WO7 BL7 VT17 VH17 WD7 VL17 BX7 MH7 NW0 ML7 CL21 NWD0 NWE0 BA6 GH2 XE7 XH7 OS0
OS1 NWF0 OE0 OS2 XL7 BO6 BD6 CH22 OE1 BA7 OS3 OE2 BO7 OS4 OE3 BD7 OE4 OS5 NS0 GL2 CL22 CH23 CL23 OS6 OE5
NSD0 OS7 CH24 GH3 GL3 OE6 OE7 CL24 NSE0 NSF0
"""
STEPS = [(word.rstrip("0123456789"), int(word.lstrip("ABCDEFGHKLMNOPSTUVWX"))) for word in ORDER.split()]


def numbered(*kinds):
    return {s: n for n, s in enumerate(x for x in STEPS if x[0] in kinds)}


W_USE = numbered("WS", "WT", "VT", "NA", "NW", "NS")
W_NORM = {"attention": W_USE["NA", 0], "swa": W_USE["NW", 0], "sb": W_USE["NS", 0], "mlp": len(W_USE)}
W_USES = len(W_USE) + 1
O_USE = numbered("BA", "WA")
O_USES = len(O_USE)
TH_USE, TL_USE, VL_USE = numbered("TH"), numbered("TL"), numbered("VL")
QK_TILES, V_TILES = len(TH_USE), len(VL_USE)
SWA_STEPS = SWA_HEADS // 4 * NB
NORMS = {"attention": 0, "swa": 1, "sb": 2, "mlp": 3}
assert W_NORM["attention"] < W_NORM["swa"] < W_NORM["sb"]
CREDIT = SPLIT_SLOTS
SPLIT_AT = {0: MLP_AT - 1, 6: MLP_AT, 7: MLP_AT + 1}
ADDS = KC - 1

TWO_PI = 2 * np.pi
ROUND = 1.5 * 2.0 ** 23
PI_BELOW = 3.1415925


def pieces(value, bits, n):
    out = []
    for _ in range(n):
        unit = 2.0 ** (np.floor(np.log2(abs(value))) - bits + 1)
        out.append(float(np.round(value / unit) * unit))
        value -= out[-1]
    return out


TWO_PI_PARTS = pieces(TWO_PI, 12, 3)


def slot_of(p):
    return (p if p < MLP_AT else p + 2) % SPLIT_SLOTS


def last_tile(p):
    if p < 0:
        return p
    if p < IN_TILES:
        return p
    if p < MLP_AT:
        return SWA_TILE + 2 * (p - SWA_OUT) + 1
    return MLP_TILE + p - MLP_AT


def free_after(p):
    if p >= MLP_AT + AHEAD:
        return MLP_TILE + p - SPLIT_SLOTS - MLP_AT
    return last_tile(max(q for q in range(p - 1, p - 3 * SPLIT_SLOTS, -1)
                         if slot_of(q if q >= 0 else q + PACKS) == slot_of(p)))



def build(nc, x_in, positions, weights, gains_in, sinks_in, inv_freq_in, out):
    with ExitStack() as ctx:
        def sb(name, shape, dtype=F32):
            return ctx.enter_context(nc.sbuf_tensor(name, shape, dtype))

        def sem(name):
            return ctx.enter_context(nc.semaphore(name))

        Z3 = ctx.enter_context(nc.psum_tensor("Z", [P, 3, T], F32))
        O = ctx.enter_context(nc.psum_tensor("O", [P, T], F32))
        D = ctx.enter_context(nc.psum_tensor("D", [P, 2, T], F32))
        W = ctx.enter_context(nc.psum_tensor("W", [P, 2, T], F32))
        Z = Z3[:, :, :].rearrange("p a b -> p (a b)")

        x = sb("x", [P, KC, T])
        xa = sb("xa", [P, 2, KC, T], F32R)
        xm = sb("xm", [P, 2, KC, T], F32R)
        stage = sb("stage", [P, 2 * PAIRS * T + 4 * Z_ALL], F32R)
        raw = sb("raw", [P, RAW_SLOTS, KC, P])
        w = sb("w", [P, SPLIT_SLOTS, 2, KC, P], F32R)
        work = sb("work", [P, Z_ALL])
        ksw = sb("ksw", [P, 2, T], F32R)
        vsw = sb("vsw", [P, NB, KV_HEADS, 2 * DH], F32R)
        probs = sb("probs", [P, 4, 2 * P])
        pt = sb("pt", [P, 2, 2, T], F32R)
        o = sb("o", [P, 2, T])
        cos = sb("cos", [P, T])
        sin = sb("sin", [P, T])
        kf = sb("kf", [P, 2, T])
        rms_a = sb("rms_a", [P, T])
        rms_w = sb("rms_w", [P, T])
        acc = sb("acc", [P, 2, T])
        other = sb("other", [P, T])
        ones = sb("ones", [P, P])
        ident_r = sb("ident_r", [P, P], F32R)
        minus_tri = sb("minus_tri", [P, P], F32R)
        minus_one = sb("minus_one", [P, P], F32R)
        strict = sb("strict", [P, P], F32R)
        band = sb("band", [P, 2 * P])
        gains = sb("gains", [P, GAINS * DEPTH + KC])
        sinks = sb("sinks", [P, DEPTH * SWA_HEADS])
        gain = sb("gain", [P, GAINS + KC])
        neg_sink = sb("neg_sink", [P, SWA_HEADS])
        inv_freq = sb("inv_freq", [P, 1])
        small = sb("small", [P, 6, 4])

        flat_m = xm[:, :, :, :].rearrange("p h c t -> p (h c t)")
        qk = flat_m[:, 0:8 * T].rearrange("p (s f t) -> p s f t", s=2, f=4)
        vst = flat_m[:, 8 * T:12 * T].rearrange("p (s j a d) -> p s j a d", s=2, j=NB, a=2)
        qsw = flat_m[:, 12 * T:16 * T].rearrange("p (j f t) -> p j f t", j=2, f=2)
        mix_sb = xa[:, :, 0:PAIRS, :]
        mix_swa = stage[:, 0:2 * PAIRS * T].rearrange("p (h c t) -> p h c t", h=2, c=PAIRS)
        sp_at = 2 * PAIRS * T
        sp = stage[:, sp_at:sp_at + 2 * Z_ALL].rearrange("p (h k) -> p h k", h=2)
        at = stage[:, sp_at + 2 * Z_ALL:].rearrange("p (h k) -> p h k", h=2)
        u = stage[:, 0:2 * KC * T].rearrange("p (h c t) -> p h c t", h=2, c=KC)
        ident = ident_r[:, :].bitcast(F32)
        flat_probs = probs[:, :, :].rearrange("p a b -> p (a b)")
        rms2 = flat_probs[:, 0:T]
        sq = [flat_probs[:, T:2 * T], rms_w[:, :]]
        sq_start = [acc[:, 0, :], rms_w[:, :], flat_probs[:, 0:T], flat_probs[:, T:2 * T],
                    acc[:, 1, :], other[:, :], o[:, 1, :], kf[:, 1, :]]
        relu = [o[:, 0, :], o[:, 1, :]]
        w_scores = W[:, :, :].rearrange("p b (i k) -> p (b i) k", i=2)
        w_heads = W[:, 0, :].rearrange("p (m d) -> p m d", d=DH)

        def v_part(kind, j, f):
            heads = vsw[:, :, :, :] if kind == "swv" else vst[:, j % 2]
            return heads.rearrange("p j a d -> p (j a) d")[:, :, f * DH:(f + 1) * DH]

        def qk_part(kind, j, f):
            return {"swk": ksw[:, f], "swq": qsw[:, j % 2, f], "sbq": qk[:, j % 2, f],
                    "sbk": qk[:, j % 2, 2 + f]}[kind]

        work0, work1 = work[:, 0:T], work[:, T:2 * T]
        scratch = {"swa": (flat_probs[:, 0:T], flat_probs[:, T:2 * T])}
        posi = other[:, :].bitcast(I32)

        raw_in = [sem(f"raw_in{i}") for i in range(RAW_SLOTS)]
        x_loaded = [sem(f"x_loaded{i}") for i in range(KC // 2)]
        positions_loaded, sinks_loaded, gains_loaded, out_stored = map(sem, (
            "positions_loaded", "sinks_loaded", "gains_loaded", "out_stored"))
        tile_done, w_full, z_full, zx_full, o_full = map(sem, ("tile_done", "w_full", "z_full", "zx_full", "o_full"))
        (w_hi, kf_hi, v_hi, sb_ln, sb_hi, z_drained, sb_ahi, swa_exp, pt_hi, o_moved, n_exp, mw_hi, mb_hi, x_hi,
         sq_full, mlp_relu, mlp_hi, trig) = map(sem, (
             "w_hi", "kf_hi", "v_hi", "sb_ln", "sb_hi", "z_drained", "sb_ahi", "swa_exp", "pt_hi", "o_moved",
             "n_exp", "mw_hi", "mb_hi", "x_hi", "sq_full", "mlp_relu", "mlp_hi", "trig"))
        (d_drained, kf_full, qk_ready, v_ready, w_drained, sb_sp, sb_split, swa_max, swa_p, pt_ready,
         o_drained, swa_o, sb_o, mw_ready, mb_ready, x_full, xa_ready, xm_ready, mlp_sq, u_ready, angle,
         start_summed, y_ready) = map(sem, (
             "d_drained", "kf_full", "qk_ready", "v_ready", "w_drained", "sb_sp", "sb_split",
             "swa_max", "swa_p", "pt_ready", "o_drained", "swa_o", "sb_o", "mw_ready", "mb_ready", "x_full",
             "xa_ready", "xm_ready", "mlp_sq", "u_ready", "angle",
             "start_summed", "y_ready"))
        w_ready, sb_alo, masks, sq_added, start_added = map(sem, ("w_ready", "sb_alo", "masks", "sq_added", "start_added"))

        x_dram = x_in.rearrange("(c p) t -> p c t", p=P)
        out_dram = out.rearrange("(c p) t -> p c t", p=P)
        block = ctx.enter_context(nc.Block())

        @block.sync
        def _(sp_):
            sp_.dma_start(posi, positions.partition_broadcast(P)).then_inc(positions_loaded, 16)
            sp_.dma_start(inv_freq[:, :], inv_freq_in).then_inc(positions_loaded, 16)
            sp_.dma_start(raw[:, 0], weights[0]).then_inc(raw_in[0], 16)
            sp_.dma_start(sinks[:, :], sinks_in.partition_broadcast(P)).then_inc(sinks_loaded, 16)
            sp_.dma_start(raw[:, 1], weights[1]).then_inc(raw_in[1], 16)
            with sp_.Fori(1, PACKS * DEPTH // RAW_SLOTS) as i:
                for n in range(RAW_SLOTS):
                    sp_.wait_ge(w_ready, (i - 1) * RAW_SLOTS + n + 1)
                    sp_.dma_start(raw[:, n], weights[bass.ds(i * RAW_SLOTS + n, 1)].rearrange("a p k -> p (a k)")
                                  ).then_inc(raw_in[n], 16)
            for n in range(PACKS * DEPTH, PACKS * DEPTH + AHEAD):
                sp_.wait_ge(w_ready, n - RAW_SLOTS + 1)
                sp_.dma_start(raw[:, n % RAW_SLOTS], weights[n]).then_inc(raw_in[n % RAW_SLOTS], 16)
            for c in range(KC):
                sp_.wait_ge(y_ready, c + 1)
                sp_.dma_start(out_dram[:, c, :], x[:, c, :]).then_inc(out_stored, 16)
            sp_.wait_ge(out_stored, 16 * KC)

        @block.tensor
        def _(pe):
            def products(p, bank, rhs, chunks, at0, first, last, ready=None):
                slot = slot_of(p)
                for i, c in enumerate(chunks):
                    if ready is not None:
                        ready(c)
                    k, start, stop = at0 + i, first and i == 0, last and i == len(chunks) - 1
                    pe.matmul(bank, w[:, slot, 0, k], rhs[:, 0, c], start=start, stop=False)
                    pe.matmul(bank, w[:, slot, 0, k], rhs[:, 1, c], start=False, stop=False)
                    mm = pe.matmul(bank, w[:, slot, 1, k], rhs[:, 0, c], start=False, stop=stop)
                return mm

            def take(l, p, tile, q=0):
                pe.wait_ge(w_ready, l * PACKS + q * 2 * KC + p + 1)
                pe.wait_ge(d_drained, l * DENSE + q * 2 * KC + tile + 1)

            def norm(l, which, ready_sem, ready):
                pe.wait_ge(ready_sem, ready)
                pe.wait_ge(w_drained, l * W_USES + W_NORM[which] + 1)
                pe.matmul(W[:, 0, :], ones[:, :], acc[:, 1 if which == "sb" else 0, :], start=True, stop=True
                          ).then_inc(w_full, 1)

            pe.sem_inc(tile_done, CREDIT)
            with pe.Fori(0, DEPTH) as l:
                for step, n in STEPS:
                    if step == "T":
                        def ready(i):
                            pe.wait_ge(xa_ready, l * KC + i + 1)
                        take(l, n, n)
                        products(n, D[:, n % 2], xa, range(KC // 2), 0, True, False, ready if n == 0 else None)
                    elif step == "U":
                        def ready(i):
                            pe.wait_ge(xa_ready, l * KC + i + 1)
                        products(n, D[:, n % 2], xa, range(KC // 2, KC), KC // 2, False, True,
                                 ready if n == 0 else None).then_inc(tile_done, 1)
                    elif step == "NA":
                        pe.wait_ge(masks, 5)
                        norm(l, "attention", sq_added, (l * 2 + 1) * ADDS)
                    elif step == "NW":
                        norm(l, "swa", swa_o, l * SWA_STEPS + SWA_STEPS)
                    elif step == "NS":
                        norm(l, "sb", sb_o, l * PAIRS + PAIRS)
                    elif step == "VT":
                        pe.wait_ge(kf_full, l * IN_TILES + n + 1)
                        pe.wait_ge(w_drained, l * W_USES + W_USE[step, n] + 1)
                        for j in range(NB):
                            mm = pe.transpose(W[:, 0, j * P:(j + 1) * P], kf[:, n % 2, j * P:(j + 1) * P], ident)
                        mm.then_inc(w_full, 1)
                    elif step == "WS":
                        pair, b = divmod(n, NB)
                        pe.wait_ge(w_drained, l * W_USES + W_USE[step, n] + 1)
                        if b == 0:
                            pe.wait_ge(qk_ready, l * QK_TILES + 1 + max(
                                TL_USE["TL", TILE_OF["swq", 2 * pair + 1]], TL_USE["TL", TILE_OF["swk", 0]]))
                        k0, at0 = (b - 1, 0) if b else (0, P)
                        for i in range(2):
                            for g in range(KV_HEADS):
                                half = slice(g * DH, (g + 1) * DH)
                                dst = W[:, g, i * 2 * P + at0:(i + 1) * 2 * P]
                                for f, (ql, kl) in enumerate(((0, 0), (0, 1), (1, 0))):
                                    mm = pe.matmul(dst, qsw[half, i, ql, b * P:(b + 1) * P],
                                                   ksw[half, kl, k0 * P:(b + 1) * P], start=f == 0, stop=f == 2)
                        mm.then_inc(w_full, 1)
                    elif step == "WT":
                        b = n % NB
                        pe.wait_ge(swa_p, l * SWA_STEPS + n + 1)
                        pe.wait_ge(w_drained, l * W_USES + W_USE[step, n] + 1)
                        for kb in (0, 1) if b else (1,):
                            for i in range(4):
                                mm = pe.transpose(W[:, kb, i * P:(i + 1) * P], probs[:, i, kb * P:(kb + 1) * P], ident)
                        mm.then_inc(w_full, 1)
                    elif step == "WA":
                        b = n % NB
                        pe.wait_ge(pt_ready, l * SWA_STEPS + n + 1)
                        pe.wait_ge(o_drained, l * O_USES + O_USE[step, n] + 1)
                        if n == 0:
                            pe.wait_ge(v_ready, l * V_TILES + VL_USE["VL", TILE_OF["swv", 0]] + 1)
                        kbs = (0, 1) if b else (1,)
                        for g in range(KV_HEADS):
                            heads = slice(g * 2 * P, (g + 1) * 2 * P)
                            for kb in kbs:
                                for f in range(2):
                                    mm = pe.matmul(O[:, heads], vsw[:, b - 1 + kb, g, :], pt[:, f, kb, heads],
                                                   start=kb == kbs[0] and f == 0, stop=kb == 1 and f == 1)
                        mm.then_inc(o_full, 1)
                    elif step == "BS":
                        par, half = n // 2 % 2, slice(n % 2 * DH, n % 2 * DH + DH)
                        pe.wait_ge(z_drained, l * SB_HEADS + n + 1)
                        if n % 2 == 0:
                            pe.wait_ge(qk_ready, l * QK_TILES + 1 + max(
                                TL_USE["TL", TILE_OF["sbk", n // 2]], TL_USE["TL", TILE_OF["sbq", n // 2]]))
                        for j in (0, 1, 3, 2):
                            dst = Z[:, Z_AT[j]:Z_AT[j] + Z_LEN[j]]
                            for f, (kl, ql) in enumerate(((2, 0), (2, 1), (3, 0))):
                                pe.matmul(dst, qk[half, par, kl, j * P:(j + 1) * P], qk[half, par, ql, j * P:T],
                                          start=f == 0 and j != 3, stop=False, skip_group_check=True)
                            mm = pe.matmul(Z[:, Z_AT[j]:Z_AT[j] + P], ident_r[:, :], strict[:, :],
                                           start=False, stop=True, skip_group_check=True)
                        mm.then_inc(z_full, 1)
                    elif step == "BX":
                        pe.wait_ge(sb_split, l * SB_HEADS + n + 1)
                        for j in (0, 1, 3, 2):
                            for jj in range(j, NB):
                                at0 = Z_AT[j] + P * (jj - j)
                                for f in range(2):
                                    mm = pe.matmul(Z[:, at0:Z_AT[j] + Z_LEN[j]],
                                                   (minus_tri if jj == j else minus_one)[:, :],
                                                   sp[:, f, Z_AT[jj]:Z_AT[jj] + Z_LEN[jj]],
                                                   start=False, stop=jj == NB - 1 and f == 1, skip_group_check=True)
                        mm.then_inc(zx_full, 1)
                    elif step == "BA":
                        pe.wait_ge(sb_alo, l * SB_HEADS + n + 1)
                        pe.wait_ge(o_drained, l * O_USES + O_USE[step, n] + 1)
                        if n % 2 == 0:
                            pe.wait_ge(v_ready, l * V_TILES + VL_USE["VL", TILE_OF["sbv", n // 2]] + 1)
                        for j in range(NB):
                            for f in range(2):
                                mm = pe.matmul(O[:, j * P:T], vst[:, n // 2 % 2, j, n % 2, :],
                                               at[:, f, Z_AT[j]:Z_AT[j] + Z_LEN[j]],
                                               start=j == 0 and f == 0, stop=j == NB - 1 and f == 1)
                        mm.then_inc(o_full, 1)
                    elif step == "OS":
                        p, tile = SWA_OUT + n // 2, SWA_TILE + n
                        take(l, p, tile)
                        if n == 0:
                            pe.wait_ge(mw_ready, l * SWA_STEPS + SWA_STEPS)
                        products(p, D[:, tile % 2], mix_swa, range(PAIRS), n % 2 * PAIRS, True, True
                                 ).then_inc(tile_done, 1)
                for d in range(KC):
                    def ready(i):
                        pe.wait_ge(mb_ready, l * PAIRS + i + 1)
                    p, tile = SB_OUT + d // 2, SB_TILE + d
                    take(l, p, tile)
                    products(p, D[:, tile % 2], mix_sb, range(PAIRS), d % 2 * PAIRS, True, True,
                             ready if d == 0 else None).then_inc(tile_done, 1)

                def quarter(q, first):
                    for c in range(KC):
                        def ready(i):
                            pe.wait_ge(xm_ready, l * KC + i + 1)
                        p, tile = MLP_AT + c, MLP_TILE + c
                        take(l, p, tile, q)
                        products(p, D[:, tile % 2], xm, range(KC), 0, True, True, ready if first and c == 0 else None
                                 ).then_inc(tile_done, 1)
                        if first and c == 2:
                            norm(l, "mlp", sq_added, (l * 2 + 2) * ADDS)
                    for d in range(KC):
                        def ready(i):
                            pe.wait_ge(u_ready, l * QUARTERS * KC + q * KC + i + 1)
                        p, tile = MLP_AT + KC + d, MLP_TILE + KC + d
                        take(l, p, tile, q)
                        products(p, D[:, tile % 2], u, range(KC), 0, True, True, ready if d == 0 else None
                                 ).then_inc(tile_done, 1)

                quarter(0, True)
                with pe.Fori(1, QUARTERS) as q:
                    quarter(q, False)
            pe.wait_ge(sq_added, (DEPTH * 2 + 1) * ADDS)
            pe.wait_ge(w_drained, DEPTH * W_USES + 1)
            pe.matmul(W[:, 0, :], ones[:, :], acc[:, 0, :], start=True, stop=True).then_inc(w_full, 1)

        @block.scalar
        def _(act):
            def split(l, p, q=0):
                n = q * 2 * KC + p
                at_layer = p % PACKS
                free = free_after(at_layer) + (DENSE if p >= PACKS else q * 2 * KC)
                act.wait_ge(raw_in[p % 2], l * (PACKS // 2 * 16) + q * (KC * 16) + (p // 2 + 1) * 16)
                act.wait_ge(tile_done, l * DENSE + free + 1 + CREDIT)
                act.activation(w[:, slot_of(at_layer), 0], raw[:, p % 2], ACT.Identity).then_inc(w_hi, 1)

            def norm_exp(use, mean, dst):
                act.wait_ge(w_drained, use + 2)
                act.activation(dst, mean, ACT.Ln)
                act.drain()
                act.activation(dst, dst, ACT.Exp, scale=-0.5).then_inc(n_exp, 1)

            def chunk_hi(dst, count, c, gain):
                act.wait_ge(x_full, count + 1)
                act.activation(dst[:, 0, c], x[:, c], ACT.Identity, scale=gain).then_inc(x_hi, 1)

            def chunk_square(past, c):
                if c == 0:
                    act.activation(acc[:, 0], x[:, c], ACT.Square)
                else:
                    act.wait_ge(sq_added, past + max(c - 2, 0))
                    act.activation(sq[c % 2], x[:, c], ACT.Square).then_inc(sq_full, 1)

            act.dma_start(gains[:, :], gains_in).then_inc(gains_loaded, 16)
            for c in range(KC):
                act.dma_start(x[:, c], x_dram[:, c]).then_inc(x_loaded[c // 2], 16)
            act.preload_act_table_set("trig_and_small")
            act.sem_inc(z_drained, 1)
            act.wait_ge(raw_in[0], 16)
            act.activation(w[:, 0, 0], raw[:, 0], ACT.Identity).then_inc(w_hi, 1)
            act.wait_ge(gains_loaded, 16)
            for c in range(KC):
                if c % 2 == 0:
                    act.wait_ge(x_loaded[c // 2], 32)
                act.activation(xa[:, 0, c], x[:, c], ACT.Identity, scale=gains[:, c:c + 1]).then_inc(x_hi, 1)
                if c == 5:
                    act.wait_ge(angle, 1)
                act.activation(sq_start[c], x[:, c], ACT.Square).then_inc(sq_full, 1)
            for p in range(1, AHEAD):
                act.wait_ge(raw_in[p % 2], (p // 2 + 1) * 16)
                act.activation(w[:, slot_of(p), 0], raw[:, p % 2], ACT.Identity).then_inc(w_hi, 1)
            act.activation(sin[:, :], sin[:, :], ACT.Sin)
            act.activation(cos[:, :], cos[:, :], ACT.Sin).then_inc(trig, 1)
            act.preload_act_table_set("natural_log_exp_and_others")
            with act.Fori(0, DEPTH) as l:
                for step, n in STEPS:
                    if step == "CH":
                        split(l, n)
                    elif step == "NAE":
                        norm_exp(l * W_USES + W_NORM["attention"], work0, work1)
                    elif step == "NSE":
                        norm_exp(l * W_USES + W_NORM["sb"], work0, work1)
                    elif step == "NWE":
                        norm_exp(l * W_USES + W_NORM["swa"], *scratch["swa"])
                    elif step == "TH":
                        kind, j = TILES[n]
                        act.wait_ge(kf_full, l * IN_TILES + n + 1)
                        if kind == "swq" and j >= 2:
                            act.wait_ge(w_full, l * W_USES + W_USE["WS", NB - 1] + 1)
                        elif kind != "swk" and j >= 2:
                            act.wait_ge(z_full, l * SB_HEADS + 2 * (j - 2) + 2)
                        act.activation(qk_part(kind, j, 0), kf[:, n % 2], ACT.Identity).then_inc(kf_hi, 1)
                    elif step == "VH":
                        kind, j = TILES[n]
                        act.wait_ge(w_full, l * W_USES + W_USE["VT", n] + 1)
                        if kind == "sbv" and j >= 2:
                            act.wait_ge(o_full, l * O_USES + O_USE["BA", 2 * (j - 2) + 1] + 1)
                        act.activation(v_part(kind, j, 0), w_heads, ACT.Identity).then_inc(v_hi, 1)
                    elif step == "BE":
                        act.wait_ge(z_full, l * SB_HEADS + n + 1)
                        if n:
                            act.wait_ge(sb_alo, l * SB_HEADS + n)
                        act.activation(work[:, :], Z[:, 0:Z_ALL], ACT.Abs)
                        act.drain()
                        act.activation(work[:, :], work[:, :], ACT.Exp, scale=-1.0)
                        act.drain()
                        act.activation(work[:, :], work[:, :], ACT.Ln, bias=1.0).then_inc(sb_ln, 1)
                    elif step == "BH":
                        act.wait_ge(sb_sp, l * SB_HEADS + n + 1)
                        act.activation(sp[:, 0], work[:, :], ACT.Identity).then_inc(sb_hi, 1)
                    elif step == "XE":
                        act.wait_ge(zx_full, l * SB_HEADS + n + 1)
                        act.activation(work[:, :], Z[:, 0:Z_ALL], ACT.Exp).then_inc(z_drained, 1)
                    elif step == "XH":
                        act.drain()
                        if n:
                            act.wait_ge(o_full, l * O_USES + O_USE["BA", n - 1] + 1)
                        act.activation(at[:, 0], work[:, :], ACT.Identity).then_inc(sb_ahi, 1)
                    elif step == "BO":
                        act.wait_ge(o_full, l * O_USES + O_USE["BA", n] + 1)
                        a, b = n % 2 * DH, (1 - n % 2) * DH
                        act.activation(other[a:a + DH, :], O[b:b + DH, :], ACT.Identity).then_inc(o_moved, 1)
                    elif step == "GH":
                        act.wait_ge(sb_o, l * PAIRS + n + 1)
                        if n == 0:
                            act.wait_ge(tile_done, l * DENSE + IN_TILES + CREDIT)
                        act.activation(mix_sb[:, 0, n], o[:, n % 2], ACT.Identity,
                                       scale=gain[:, KC + n:KC + n + 1]).then_inc(mb_hi, 1)
                    elif step == "WE":
                        act.wait_ge(swa_max, l * SWA_STEPS + n + 1)
                        at0 = 0 if n % NB else P
                        for i in range(4):
                            act.activation(probs[:, i, at0:], probs[:, i, at0:], ACT.Exp, bias=small[:, 0, i:i + 1],
                                           accum_out=small[:, 3, i:i + 1])
                        act.activation(small[:, 2, :], small[:, 1, :], ACT.Exp).then_inc(swa_exp, 1)
                    elif step == "WH":
                        act.wait_ge(w_full, l * W_USES + W_USE["WT", n] + 1)
                        kb = 0 if n % NB else 1
                        if n:
                            act.wait_ge(o_full, l * O_USES + O_USE["WA", n - 1] + 1)
                        act.activation(pt[:, 0, kb:], W[:, kb:], ACT.Identity).then_inc(pt_hi, 1)
                    elif step == "WO":
                        act.wait_ge(o_full, l * O_USES + O_USE["WA", n] + 1)
                        act.activation(other[0:DH, 0:2 * P], O[DH:P, 0:2 * P], ACT.Identity)
                        act.activation(other[DH:P, 0:2 * P], O[0:DH, 2 * P:T], ACT.Identity).then_inc(o_moved, 1)
                    elif step == "MH":
                        pair, b = divmod(n, NB)
                        act.wait_ge(swa_o, l * SWA_STEPS + n + 1)
                        for i in range(2):
                            e = 2 * pair + i
                            last = act.activation(mix_swa[:, 0, e, b * P:(b + 1) * P], other[:, i * P:(i + 1) * P],
                                                  ACT.Identity, scale=gain[:, KC + PAIRS + e:KC + PAIRS + e + 1])
                        last.then_inc(mw_hi, 1)
                for d in range(KC):
                    if d in SPLIT_AT:
                        split(l, SPLIT_AT[d])
                    chunk_hi(xm, l * 2 * KC + d, d, gain[:, 2 * KC + d:2 * KC + d + 1])
                    chunk_square((l * 2 + 1) * ADDS, d)
                split(l, MLP_AT + 2)

                def quarter(q, first, last):
                    for c in range(KC):
                        split(l, MLP_AT + c + AHEAD, q)
                        act.wait_ge(tile_done, l * DENSE + q * 2 * KC + MLP_TILE + c + 1 + CREDIT)
                        act.activation(relu[c % 2], D[:, (MLP_TILE + c) % 2], ACT.Relu).then_inc(mlp_relu, 1)
                        act.wait_ge(mlp_sq, l * QUARTERS * KC + q * KC + c + 1)
                        act.activation(u[:, 0, c], kf[:, c % 2], ACT.Identity).then_inc(mlp_hi, 1)
                        if first and c == 3:
                            norm_exp(l * W_USES + W_NORM["mlp"], work0, work1)
                    for d in range(KC):
                        if last and d >= KC - AHEAD:
                            split(l, PACKS + d - (KC - AHEAD))
                        else:
                            split(l, MLP_AT + KC + d + AHEAD, q)
                        if last:
                            act.wait_ge(x_full, l * 2 * KC + KC + d + 1)
                            if d == KC - 1:
                                chunk_square((l * 2 + 2) * ADDS, d)
                            chunk_hi(xa, l * 2 * KC + KC + d, d, gain[:, GAINS + d:GAINS + d + 1])
                            if d < KC - 1:
                                chunk_square((l * 2 + 2) * ADDS, d)

                quarter(0, True, False)
                with act.Fori(1, QUARTERS - 1) as q:
                    quarter(q, False, False)
                quarter(QUARTERS - 1, False, True)
            norm_exp(DEPTH * W_USES, work0, work1)

        @block.gpsimd
        def _(pool):
            def split(n, p):
                pool.wait_ge(w_hi, n + 1)
                slot = slot_of(p)
                pool.tensor_tensor(w[:, slot, 1], raw[:, p % 2], w[:, slot, 0].bitcast(F32), ALU.subtract
                                   ).then_inc(w_ready, 1)

            def add_squares(past, c):
                if c:
                    pool.wait_ge(sq_full, past + c + 1)
                    pool.tensor_tensor(acc[:, 0], acc[:, 0], sq[c % 2], ALU.add)
                    pool.drain().then_inc(sq_added, 1)

            def constant(dst, value, fill, compare, base, step, channel):
                pool.memset(dst, value)
                pool.drain()
                pool.affine_select(out=dst, in_=dst, compare_op=compare, fill=fill, base=base,
                                   pattern=[[step, dst.shape[1]]], channel_multiplier=channel)
                pool.drain()

            pool.memset(ones[:, :], 1.0)
            diag, tri, row, low = (o[:, 0, i * P:(i + 1) * P] for i in range(4))
            constant(diag, 0.0, 1.0, ALU.not_equal, 0, -1, 1)
            constant(tri, -1.0, 0.0, ALU.is_ge, 0, -1, 1)
            constant(low, 0.0, NEG, ALU.is_gt, 0, 1, -1)
            pool.memset(row, -1.0)
            constant(band[:, :], 0.0, NEG, ALU.is_ge, P, -1, 1)
            pool.affine_select(out=band[:, :], in_=band[:, :], compare_op=ALU.is_gt, fill=NEG, base=0,
                               pattern=[[1, 2 * P]], channel_multiplier=-1).then_inc(masks, 1)
            pool.drain()
            for dst, src in ((ident_r, diag), (minus_tri, tri), (minus_one, row), (strict, low)):
                pool.tensor_copy(dst[:, :], src).then_inc(masks, 1)
            split(0, 0)
            for c in range(1, KC // 2):
                pool.wait_ge(sq_full, c + 1)
                pool.tensor_tensor(acc[:, 0], acc[:, 0], sq_start[c], ALU.add)
                pool.drain()
            pool.drain().then_inc(start_added, 1)
            for p in range(1, AHEAD):
                split(p, p)
                if p == 1:
                    pool.wait_ge(start_summed, 1)
                    pool.sem_inc(sq_added, ADDS)
            with pool.Fori(0, DEPTH) as l:
                for step, n in STEPS:
                    if step == "CL":
                        split(l * PACKS + n, n)
                    elif step == "XL":
                        pool.wait_ge(sb_ahi, l * SB_HEADS + n + 1)
                        pool.tensor_tensor(at[:, 1], work[:, :], at[:, 0].bitcast(F32), ALU.subtract
                                           ).then_inc(sb_alo, 1)
                for d in range(KC):
                    if d in SPLIT_AT:
                        split(l * PACKS + SPLIT_AT[d], SPLIT_AT[d])
                    add_squares((l * 2 + 1) * ADDS, d)
                split(l * PACKS + MLP_AT + 2, MLP_AT + 2)
                with pool.Fori(0, QUARTERS - 1) as q:
                    for p in range(MLP_AT + AHEAD, MLP_AT + AHEAD + 2 * KC):
                        split(l * PACKS + q * 2 * KC + p, p)
                for c in range(KC):
                    p = MLP_AT + c + AHEAD
                    split(l * PACKS + (QUARTERS - 1) * 2 * KC + p, p)
                for d in range(KC):
                    p = MLP_AT + KC + d + AHEAD
                    if d >= KC - AHEAD:
                        split(l * PACKS + PACKS + d - (KC - AHEAD), d - (KC - AHEAD))
                    else:
                        split(l * PACKS + (QUARTERS - 1) * 2 * KC + p, p)
                    add_squares((l * 2 + 2) * ADDS, d)

        @block.vector
        def _(dve):
            def norm_mean(l, use, width, mean):
                dve.wait_ge(w_full, l * W_USES + use + 1)
                dve.tensor_scalar(mean, W[:, 0, :], 1.0 / width, EPS, ALU.mult, ALU.add).then_inc(w_drained, 1)

            def norm_refine(count, mean, guess, dst):
                dve.wait_ge(n_exp, count + 1)
                dve.scalar_tensor_tensor(dst, mean, -0.5, guess, ALU.mult, ALU.mult)
                dve.drain()
                dve.tensor_tensor(dst, dst, guess, ALU.mult)
                dve.drain()
                dve.scalar_tensor_tensor(dst, dst, 1.5, guess, ALU.add, ALU.mult)
                dve.drain()

            def chunk_lo(dst, count, c, gain, ready):
                dve.wait_ge(x_hi, count + 1)
                dve.scalar_tensor_tensor(dst[:, 1, c], x[:, c], gain, dst[:, 0, c].bitcast(F32), ALU.mult,
                                         ALU.subtract).then_inc(ready, 1)

            dve.wait_ge(positions_loaded, 32)
            dve.tensor_copy(kf[:, 0], posi)
            dve.drain()
            dve.tensor_scalar(sin[:, :], kf[:, 0], inv_freq[:, 0:1], None, ALU.mult)
            dve.drain()
            dve.tensor_scalar(kf[:, 0], sin[:, :], 1.0 / TWO_PI, ROUND, ALU.mult, ALU.add)
            dve.drain()
            dve.tensor_scalar(kf[:, 0], kf[:, 0], ROUND, None, ALU.subtract)
            dve.drain()
            dve.tensor_scalar(kf[:, 1], kf[:, 0], ROUND * 2048, None, ALU.add)
            dve.drain()
            dve.tensor_scalar(kf[:, 1], kf[:, 1], ROUND * 2048, None, ALU.subtract)
            dve.drain()
            dve.tensor_tensor(kf[:, 0], kf[:, 0], kf[:, 1], ALU.subtract)
            dve.drain()
            for part in TWO_PI_PARTS:
                for k in (1, 0):
                    dve.scalar_tensor_tensor(sin[:, :], kf[:, k], -part, sin[:, :], ALU.mult, ALU.add)
                    dve.drain()
            dve.tensor_scalar(sin[:, :], sin[:, :], PI_BELOW, -PI_BELOW, ALU.min, ALU.max)
            dve.drain()
            dve.scalar_tensor_tensor(cos[:, :], sin[:, :], -1.0, sin[:, :], ALU.mult, ALU.min)
            dve.drain()
            dve.tensor_scalar(cos[:, :], cos[:, :], float(np.float32(np.pi / 2)), None, ALU.add).then_inc(angle, 1)
            dve.wait_ge(gains_loaded, 16)
            dve.sem_inc(d_drained, 2)
            dve.sem_inc(w_drained, 1)
            dve.sem_inc(o_drained, 1)
            for c in range(KC):
                chunk_lo(xa, c, c, gains[:, c:c + 1], xa_ready)
            for c in range(KC // 2 + 1, KC):
                dve.wait_ge(sq_full, c + 1)
                dve.tensor_tensor(acc[:, 1], acc[:, 1], sq_start[c], ALU.add)
                dve.drain()
            dve.wait_ge(start_added, 1)
            dve.tensor_tensor(acc[:, 0], acc[:, 0], acc[:, 1], ALU.add)
            dve.drain().then_inc(start_summed, 1)
            dve.wait_ge(sinks_loaded, 16)
            dve.wait_ge(masks, 5)

            with dve.Fori(0, DEPTH) as l:
                dve.drain()
                dve.tensor_copy(gain[:, :], gains[:, bass.ds(l * GAINS, GAINS + KC)])
                dve.tensor_scalar(neg_sink[:, :], sinks[:, bass.ds(l * SWA_HEADS, SWA_HEADS)], -1.0, None, ALU.mult)
                dve.drain()
                for step, n in STEPS:
                    if step == "NAD":
                        norm_mean(l, W_NORM["attention"], DM, work0)
                    elif step == "NAF":
                        norm_refine(l * len(NORMS) + NORMS["attention"], work0, work1, rms_a[:, :])
                    elif step == "NSD":
                        norm_mean(l, W_NORM["sb"], SB_W, work0)
                    elif step == "NSF":
                        norm_refine(l * len(NORMS) + NORMS["sb"], work0, work1, rms_a[:, :])
                    elif step == "NWD":
                        norm_mean(l, W_NORM["swa"], SWA_W, scratch["swa"][0])
                    elif step == "NWF":
                        norm_refine(l * len(NORMS) + NORMS["swa"], *scratch["swa"], rms_w[:, :])
                    elif step == "TE":
                        kind, j = TILES[n]
                        src = kf[:, n % 2]
                        dve.wait_ge(tile_done, l * DENSE + n + 1 + CREDIT)
                        scale = SCALE if kind in ("sbq", "swq") else 1.0
                        dve.scalar_tensor_tensor(src, D[:, n % 2], scale, rms_a[:, :], ALU.mult, ALU.mult
                                                 ).then_inc(d_drained, 1)
                        if kind in ("swk", "swq"):
                            if (kind, j) == ("swk", 0):
                                dve.wait_ge(trig, 1)
                            dve.drain()
                            for a in range(4):
                                b = a ^ 1
                                dve.tensor_tensor(rms_w[b * 32:b * 32 + 32, :], kf[a * 32:a * 32 + 32, n % 2],
                                                  sin[a * 32:a * 32 + 32, :], ALU.mult)
                            dve.drain()
                            dve.tensor_tensor(src, src, cos[:, :], ALU.mult)
                            dve.drain()
                            dve.tensor_tensor(src, src, rms_w[:, :], ALU.add)
                        dve.drain().then_inc(kf_full, 1)
                    elif step == "TL":
                        kind, j = TILES[n]
                        dve.wait_ge(kf_hi, l * QK_TILES + TH_USE["TH", n] + 1)
                        dve.tensor_tensor(qk_part(kind, j, 1), kf[:, n % 2], qk_part(kind, j, 0).bitcast(F32),
                                          ALU.subtract).then_inc(qk_ready, 1)
                        dve.drain()
                    elif step == "VL":
                        kind, j = TILES[n]
                        dve.wait_ge(v_hi, l * V_TILES + VL_USE["VL", n] + 1)
                        dve.tensor_tensor(v_part(kind, j, 1), w_heads, v_part(kind, j, 0).bitcast(F32), ALU.subtract
                                          ).then_inc(v_ready, 1)
                        dve.drain().then_inc(w_drained, 1)
                    elif step == "BP":
                        dve.wait_ge(sb_ln, l * SB_HEADS + n + 1)
                        dve.scalar_tensor_tensor(work[:, :], Z[:, 0:Z_ALL], 0.0, work[:, :], ALU.max, ALU.add
                                                 ).then_inc(sb_sp, 1)
                    elif step == "BL":
                        dve.wait_ge(sb_hi, l * SB_HEADS + n + 1)
                        dve.tensor_tensor(sp[:, 1], work[:, :], sp[:, 0].bitcast(F32), ALU.subtract
                                          ).then_inc(sb_split, 1)
                    elif step == "BD":
                        dve.wait_ge(o_moved, l * O_USES + O_USE["BA", n] + 1)
                        a, pair = n % 2 * DH, n // 2
                        last = dve.tensor_tensor(o[a:a + DH, pair % 2], O[a:a + DH, :], other[a:a + DH, :], ALU.add)
                        if n % 2:
                            dve.drain()
                            if pair == 0:
                                dve.tensor_tensor(acc[:, 1], o[:, 0], o[:, 0], ALU.mult)
                            else:
                                dve.tensor_tensor(other[:, :], o[:, pair % 2], o[:, pair % 2], ALU.mult)
                                dve.drain()
                                dve.tensor_tensor(acc[:, 1], acc[:, 1], other[:, :], ALU.add)
                            dve.drain().then_inc(sb_o, 1)
                        dve.drain().then_inc(o_drained, 1)
                    elif step == "GL":
                        dve.wait_ge(mb_hi, l * PAIRS + n + 1)
                        dve.scalar_tensor_tensor(mix_sb[:, 1, n], o[:, n % 2], gain[:, KC + n:KC + n + 1],
                                                 mix_sb[:, 0, n].bitcast(F32), ALU.mult, ALU.subtract
                                                 ).then_inc(mb_ready, 1)
                        dve.drain()
                    elif step == "WK":
                        at0 = 0 if n % NB else P
                        dve.wait_ge(w_full, l * W_USES + W_USE["WS", n] + 1)
                        dve.tensor_tensor(probs[:, :, at0:], w_scores[:, :, at0:],
                                          band[:, at0:].unsqueeze(1).to_broadcast([P, 4, 2 * P - at0]),
                                          ALU.add).then_inc(w_drained, 1)
                        dve.drain()
                    elif step == "WM":
                        at0 = 0 if n % NB else P
                        s = neg_sink[:, n // NB * 4:n // NB * 4 + 4]
                        dve.tensor_reduce(small[:, 5, :], probs[:, :, at0:], AX.X, ALU.max)
                        dve.drain()
                        dve.scalar_tensor_tensor(small[:, 0, :], small[:, 5, :], -1.0, s, ALU.mult, ALU.min)
                        dve.drain()
                        dve.tensor_tensor(small[:, 1, :], small[:, 0, :], s, ALU.subtract).then_inc(swa_max, 1)
                    elif step == "WN":
                        at0 = 0 if n % NB else P
                        dve.wait_ge(swa_exp, l * SWA_STEPS + n + 1)
                        dve.tensor_tensor(small[:, 4, :], small[:, 3, :], small[:, 2, :], ALU.add)
                        dve.drain()
                        dve.reciprocal(small[:, 4, :], small[:, 4, :])
                        dve.drain()
                        for i in range(4):
                            last = dve.tensor_scalar(probs[:, i, at0:], probs[:, i, at0:], small[:, 4, i:i + 1], None,
                                                     ALU.mult)
                        last.then_inc(swa_p, 1)
                    elif step == "WL":
                        kb = 0 if n % NB else 1
                        dve.wait_ge(pt_hi, l * SWA_STEPS + n + 1)
                        dve.tensor_tensor(pt[:, 1, kb:], W[:, kb:], pt[:, 0, kb:].bitcast(F32), ALU.subtract
                                          ).then_inc(pt_ready, 1)
                        dve.drain().then_inc(w_drained, 1)
                    elif step == "WD":
                        pair, b = divmod(n, NB)
                        dve.wait_ge(o_moved, l * O_USES + O_USE["WA", n] + 1)
                        for g in range(KV_HEADS):
                            rows = slice(g * DH, (g + 1) * DH)
                            dve.tensor_tensor(other[rows, 0:2 * P], O[rows, g * 2 * P:(g + 1) * 2 * P],
                                              other[rows, 0:2 * P], ALU.add)
                        dve.drain()
                        dve.tensor_tensor(other[:, 2 * P:T], other[:, 0:2 * P], other[:, 0:2 * P], ALU.mult)
                        dve.drain()
                        total = acc[:, 0, b * P:(b + 1) * P]
                        if pair == 0:
                            dve.tensor_tensor(total, other[:, 2 * P:3 * P], other[:, 3 * P:T], ALU.add)
                        else:
                            for i in range(2):
                                dve.tensor_tensor(total, total, other[:, (2 + i) * P:(3 + i) * P], ALU.add)
                                dve.drain()
                        dve.drain().then_inc(swa_o, 1)
                    elif step == "ML":
                        pair, b = divmod(n, NB)
                        dve.wait_ge(mw_hi, l * SWA_STEPS + n + 1)
                        for i in range(2):
                            e, tokens = 2 * pair + i, slice(b * P, (b + 1) * P)
                            last = dve.scalar_tensor_tensor(
                                mix_swa[:, 1, e, tokens], other[:, i * P:(i + 1) * P],
                                gain[:, KC + PAIRS + e:KC + PAIRS + e + 1], mix_swa[:, 0, e, tokens].bitcast(F32),
                                ALU.mult, ALU.subtract)
                        last.then_inc(mw_ready, 1)
                        dve.drain().then_inc(o_drained, 1)
                    elif step == "OE":
                        tile = SWA_TILE + n
                        dve.wait_ge(tile_done, l * DENSE + tile + 1 + CREDIT)
                        dve.tensor_tensor(kf[:, 0], D[:, tile % 2], rms_w[:, :], ALU.mult).then_inc(d_drained, 1)
                        dve.drain()
                        dve.tensor_tensor(x[:, n], x[:, n], kf[:, 0], ALU.add)
                        dve.drain()
                for d in range(KC):
                    tile = SB_TILE + d
                    dve.wait_ge(tile_done, l * DENSE + tile + 1 + CREDIT)
                    dve.tensor_tensor(kf[:, 0], D[:, tile % 2], rms_a[:, :], ALU.mult).then_inc(d_drained, 1)
                    dve.drain()
                    dve.tensor_tensor(x[:, d], x[:, d], kf[:, 0], ALU.add)
                    dve.drain().then_inc(x_full, 1)
                    if d:
                        chunk_lo(xm, l * 2 * KC + KC + d - 1, d - 1,
                                 gain[:, 2 * KC + d - 1:2 * KC + d], xm_ready)
                chunk_lo(xm, l * 2 * KC + 2 * KC - 1, KC - 1, gain[:, 3 * KC - 1:3 * KC], xm_ready)

                def quarter(q, first, last):
                    for c in range(KC):
                        count = l * QUARTERS * KC + q * KC + c
                        dve.wait_ge(mlp_relu, count + 1)
                        dve.tensor_tensor(kf[:, c % 2], relu[c % 2], relu[c % 2], ALU.mult).then_inc(mlp_sq, 1)
                        dve.sem_inc(d_drained, 1)
                        dve.wait_ge(mlp_hi, count + 1)
                        dve.tensor_tensor(u[:, 1, c], kf[:, c % 2], u[:, 0, c].bitcast(F32), ALU.subtract
                                          ).then_inc(u_ready, 1)
                        dve.drain()
                        if first and c == 3:
                            norm_mean(l, W_NORM["mlp"], DM, work0)
                            norm_refine(l * len(NORMS) + NORMS["mlp"], work0, work1, rms2)
                            dve.tensor_tensor(rms2, rms2, rms2, ALU.mult)
                            dve.drain()
                    for d in range(KC):
                        tile = MLP_TILE + KC + d
                        dve.wait_ge(tile_done, l * DENSE + q * 2 * KC + tile + 1 + CREDIT)
                        dve.tensor_tensor(other[:, :], D[:, tile % 2], rms2, ALU.mult).then_inc(d_drained, 1)
                        dve.drain()
                        done = dve.tensor_tensor(x[:, d], x[:, d], other[:, :], ALU.add)
                        if last:
                            dve.drain().then_inc(x_full, 1)
                            chunk_lo(xa, l * 2 * KC + 2 * KC + d, d, gain[:, GAINS + d:GAINS + d + 1],
                                     xa_ready)
                        else:
                            dve.drain()

                quarter(0, True, False)
                with dve.Fori(1, QUARTERS - 1) as q:
                    quarter(q, False, False)
                quarter(QUARTERS - 1, False, True)
            norm_mean(DEPTH, 0, DM, work0)
            norm_refine(DEPTH * len(NORMS), work0, work1, rms_a[:, :])
            for c in range(KC):
                dve.scalar_tensor_tensor(x[:, c], x[:, c], gains[:, DEPTH * GAINS + c:DEPTH * GAINS + c + 1],
                                         rms_a[:, :], ALU.mult, ALU.mult).then_inc(y_ready, 1)


def kernel(**inputs):
    import concourse.bacc as bacc
    from concourse.bass_utils import run_bass_kernel_spmd
    a = {k: np.ascontiguousarray(v) for k, v in inputs.items()}

    group = SWA_HEADS // KV_HEADS
    pairs = [h for e in range(PAIRS) for h in (e, group + e)]
    swa_rows = np.concatenate([np.arange(h * DH, (h + 1) * DH) for h in pairs])
    in_columns = np.arange(a["w_in"].shape[2])
    in_columns[3 * SB_W:3 * SB_W + SWA_W] = 3 * SB_W + swa_rows

    def pack(part):
        return part.reshape(KC, P, P).transpose(1, 0, 2)

    order, gains, sinks = [], [], []
    for l in range(DEPTH):
        w_in, w_out, w_up, w_down = a["w_in"][l][:, in_columns], a["w_out"][l], a["w_up"][l], a["w_down"][l]
        for kind, j in TILES:
            m = COLUMN_BLOCK[kind] + j
            order.append(pack(w_in[:, m * P:(m + 1) * P]))
        for rows in (SB_W + swa_rows, np.arange(SB_W)):
            for k in range(OUT_PACKS):
                order.append(pack(np.concatenate([w_out[rows, d * P:(d + 1) * P] for d in (2 * k, 2 * k + 1)])))
        for q in range(QUARTERS):
            for c in range(KC):
                order.append(pack(w_up[:, (q * KC + c) * P:(q * KC + c + 1) * P]))
            for d in range(KC):
                order.append(pack(w_down[q * DM:(q + 1) * DM, d * P:(d + 1) * P]))
        gains += [a["attn_norm"][l], a["sb_norm"][l], a["swa_norm"][l][swa_rows], a["mlp_norm"][l]]
        sinks += [a["sinks"][l][[g * group + 2 * t + i for t in range(group // 2) for g in range(KV_HEADS)
                                 for i in range(2)]]]
    order += order[:AHEAD]
    weights = np.stack(order).reshape(PACKS * DEPTH + AHEAD, P, KC * P)
    gains = np.concatenate(gains + [a["final_norm"]]).reshape(-1, P).T
    half = DH // 2
    inv_freq = np.tile((1.0 / (THETA ** (np.arange(half) * (2.0 / DH)))).astype(np.float32), P // half)[:, None]
    inv_freq[(np.arange(P) // half) % 2 == 1] *= -1
    arrays = {
        "in_x": a["x"][0].T, "in_positions": a["positions"][None, :], "in_weights": weights, "in_gains": gains,
        "in_sinks": np.concatenate(sinks)[None, :], "in_inv_freq": inv_freq,
    }
    arrays = {k: np.ascontiguousarray(v) for k, v in arrays.items()}
    nc = bacc.Bacc("TRN2", target_bir_lowering=False, num_devices=1)
    args = [nc.dram_tensor(k, v.shape, mybir.dt.from_np(v.dtype), kind="ExternalInput").ap() for k, v in arrays.items()]
    args.append(nc.dram_tensor("out_x", (DM, T), F32, kind="ExternalOutput").ap())
    build(nc, *args)
    r = run_bass_kernel_spmd(nc, [arrays], core_ids=[0])
    return np.ascontiguousarray(r.results[0]["out_x"].T)[None]
```
